# Optimizing a Trainium2 kernel written in Bass

```python
import math
import jax, jax.numpy as jnp
from jax import lax
import numpy as np

D_MODEL = 1024
BATCH = 1
SEQ = 512
DEPTH = 1

CHUNK = 64
HEAD_DIM = 64
D_MIX = D_MODEL
N_MIXERS = 4
D_GROUP = D_MIX // N_MIXERS

POOL_WINDOWS = (2, 4, 8, 16)
POOL_GROUPS = len(POOL_WINDOWS)
POOL_CH = D_GROUP // POOL_GROUPS

B_HEADS = D_GROUP // HEAD_DIM
B_LEFT_CHUNKS = 8
B_BAND = (B_LEFT_CHUNKS + 1) * CHUNK
REL_CLIP = 128

C_HEADS = D_GROUP // HEAD_DIM
C_KV_HEADS = 2
C_GRP = C_HEADS // C_KV_HEADS
C_WINDOW = 128
C_WIN_CHUNKS = C_WINDOW // CHUNK
C_BAND = C_WIN_CHUNKS * CHUNK

SGU_GROUPS = 4
SGU_CH = D_GROUP // SGU_GROUPS
SGU_LEN = 128

IN_WIDTHS = (D_GROUP,
             D_GROUP, D_GROUP, D_GROUP,
             C_HEADS * HEAD_DIM, C_KV_HEADS * HEAD_DIM, C_KV_HEADS * HEAD_DIM,
             D_GROUP, D_GROUP)
D_IN = sum(IN_WIDTHS)
IN_SPLITS = [int(s) for s in np.cumsum(IN_WIDTHS)[:-1]]

PEER_HEADS = 8
N_KEYS = 128
N_EXPERTS = N_KEYS * N_KEYS
PEER_TOPK = 16
D_QUERY = 256
D_SUBKEY = D_QUERY // 2
PEER_BLOCK = 128

ALPHA = (2 * DEPTH) ** 0.25
BETA = (8 * DEPTH) ** -0.25
LN_EPS = 1e-5
NEG = -1e30

kernel_name = "hybrid_streaming_pool_attn_sgu_peer"

def layer_norm(x, g, b):
    xf = x.astype(jnp.float32)
    mu = jnp.mean(xf, axis=-1, keepdims=True)
    var = jnp.mean(jnp.square(xf - mu), axis=-1, keepdims=True)
    return ((xf - mu) * lax.rsqrt(var + LN_EPS) * g + b).astype(x.dtype)

def pool_mixer(a, lin, scale):
    bsz, s_len, _ = a.shape
    af = a.astype(jnp.float32)
    csum = jnp.cumsum(af, axis=1)
    t = jnp.arange(s_len)
    outs = []
    for g, w in enumerate(POOL_WINDOWS):
        sl = slice(g * POOL_CH, (g + 1) * POOL_CH)
        cs = jnp.pad(csum[:, :, sl], ((0, 0), (w, 0), (0, 0)))
        win_sum = cs[:, w:] - cs[:, :s_len]
        count = jnp.minimum(t + 1, w).astype(jnp.float32)[None, :, None]
        outs.append(win_sum / count - af[:, :, sl])
    p = jnp.stack(outs, axis=2).astype(a.dtype)
    y = jnp.einsum('bsgc,gcd->bsgd', p, lin).reshape(bsz, s_len, D_GROUP)
    return y * scale

def chunk_band(t, n_left):
    bsz, s_len, h, dh = t.shape
    nc = s_len // CHUNK
    tc = t.reshape(bsz, nc, CHUNK, h, dh)
    tp = jnp.pad(tc, ((0, 0), (n_left, 0), (0, 0), (0, 0), (0, 0)))
    band = jnp.stack([tp[:, j:j + nc] for j in range(n_left + 1)], axis=2)
    return band.reshape(bsz, nc, (n_left + 1) * CHUNK, h, dh)

def band_valid(nc, n_left):
    c = jnp.arange(nc)[:, None]
    j = jnp.arange((n_left + 1) * CHUNK)[None, :] // CHUNK
    return (c - n_left + j) >= 0

def chunk_relpos_attention(q, k, v, rel_bias):
    bsz, s_len, h, dh = q.shape
    nc = s_len // CHUNK
    qc = q.reshape(bsz, nc, CHUNK, h, dh)
    kb = chunk_band(k, B_LEFT_CHUNKS)
    vb = chunk_band(v, B_LEFT_CHUNKS)
    s = jnp.einsum('bnihd,bnphd->bnhip', qc, kb).astype(jnp.float32) * (dh ** -0.5)
    i = jnp.arange(CHUNK)[:, None]
    p = jnp.arange(B_BAND)[None, :]
    rel = B_LEFT_CHUNKS * CHUNK + i - p
    idx = jnp.clip(rel, -REL_CLIP, REL_CLIP) + REL_CLIP
    bias = rel_bias[:, idx].astype(jnp.float32)
    valid = band_valid(nc, B_LEFT_CHUNKS)
    s = jnp.where(valid[None, :, None, None, :], s + bias[None, None], NEG)
    prob = jax.nn.softmax(s, axis=-1).astype(v.dtype)
    o = jnp.einsum('bnhip,bnphd->bnihd', prob, vb)
    return o.reshape(bsz, s_len, h * dh)

def alibi_slopes(n_heads):
    return 2.0 ** (-8.0 * (jnp.arange(n_heads, dtype=jnp.float32) + 1.0) / n_heads)

def swa_sink_attention(q, k, v, sinks):
    bsz, s_len, hq, dh = q.shape
    nc = s_len // CHUNK
    qc = q.reshape(bsz, nc, CHUNK, C_KV_HEADS, C_GRP, dh)
    kb = chunk_band(k, C_WIN_CHUNKS - 1)
    vb = chunk_band(v, C_WIN_CHUNKS - 1)
    s = jnp.einsum('bnikgd,bnpkd->bnkgip', qc, kb).astype(jnp.float32) * (dh ** -0.5)
    i = jnp.arange(CHUNK)[:, None]
    p = jnp.arange(C_BAND)[None, :]
    dist = jnp.abs((C_WIN_CHUNKS - 1) * CHUNK + i - p).astype(jnp.float32)
    alibi = (-alibi_slopes(hq)[:, None, None] * dist).reshape(C_KV_HEADS, C_GRP, CHUNK, C_BAND)
    valid = band_valid(nc, C_WIN_CHUNKS - 1)
    s = jnp.where(valid[None, :, None, None, None, :], s + alibi[None, None], NEG)
    sink = sinks.astype(jnp.float32).reshape(C_KV_HEADS, C_GRP)[None, None, :, :, None, None]
    m = jnp.maximum(jnp.max(s, axis=-1, keepdims=True), sink)
    e = jnp.exp(s - m)
    prob = (e / (jnp.sum(e, axis=-1, keepdims=True) + jnp.exp(sink - m))).astype(v.dtype)
    o = jnp.einsum('bnkgip,bnpkd->bnikgd', prob, vb)
    return o.reshape(bsz, s_len, hq * dh)

def spatial_gating(u, v, ln_g, ln_b, w_s, b_s):
    bsz, s_len, _ = u.shape
    nb = s_len // SGU_LEN
    v = layer_norm(v, ln_g, ln_b).reshape(bsz, nb, SGU_LEN, SGU_GROUPS, SGU_CH)
    mask = jnp.tril(jnp.ones((SGU_LEN, SGU_LEN), dtype=bool))
    w = jnp.where(mask[None], w_s, 0.0)
    mixed = jnp.einsum('gts,bnsgc->bntgc', w, v) + b_s.T[None, None, :, :, None]
    return (u.reshape(bsz, nb, SGU_LEN, SGU_GROUPS, SGU_CH) * mixed).reshape(bsz, s_len, D_GROUP)

def peer_ffn(x, w_q, sub_keys, expert_u, expert_v):
    bsz, s_len, d = x.shape
    xt = x.reshape(-1, d)
    n_tok = xt.shape[0]
    q = (xt @ w_q).reshape(n_tok, PEER_HEADS, 2, D_SUBKEY)
    sc = jnp.einsum('thzd,hznd->thzn', q, sub_keys).astype(jnp.float32)
    top_v, top_i = lax.top_k(sc, PEER_TOPK)
    cand_s = top_v[:, :, 0, :, None] + top_v[:, :, 1, None, :]
    cand_i = top_i[:, :, 0, :, None] * N_KEYS + top_i[:, :, 1, None, :]
    cand_s = cand_s.reshape(n_tok, PEER_HEADS, PEER_TOPK * PEER_TOPK)
    cand_i = cand_i.reshape(n_tok, PEER_HEADS, PEER_TOPK * PEER_TOPK)
    best_s, pos = lax.top_k(cand_s, PEER_TOPK)
    e_idx = jnp.take_along_axis(cand_i, pos, axis=-1)
    gate = jax.nn.softmax(best_s, axis=-1).astype(x.dtype)
    nblk = n_tok // PEER_BLOCK

    def block(args):
        xb, idx, g = args
        hidden = jnp.einsum('pd,pkd->pk', xb, expert_u[idx])
        act = jax.nn.gelu(hidden.astype(jnp.float32), approximate=False).astype(xb.dtype)
        return jnp.einsum('pk,pkd->pd', g * act, expert_v[idx])

    y = lax.map(block, (xt.reshape(nblk, PEER_BLOCK, d),
                        e_idx.reshape(nblk, PEER_BLOCK, PEER_HEADS * PEER_TOPK),
                        gate.reshape(nblk, PEER_BLOCK, PEER_HEADS * PEER_TOPK)))
    return y.reshape(bsz, s_len, d)

def hybrid_mixer(x, w_in, w_out, pool_lin, pool_scale, rel_bias, sinks,
                 sgu_ln_g, sgu_ln_b, sgu_w, sgu_b):
    bsz, s_len, _ = x.shape
    h = x @ w_in
    a, bq, bk, bv, cq, ck, cv, du, dv = jnp.split(h, IN_SPLITS, axis=-1)
    y_a = pool_mixer(a, pool_lin, pool_scale)
    heads = lambda t, n: t.reshape(bsz, s_len, n, HEAD_DIM)
    y_b = chunk_relpos_attention(heads(bq, B_HEADS), heads(bk, B_HEADS), heads(bv, B_HEADS), rel_bias)
    y_c = swa_sink_attention(heads(cq, C_HEADS), heads(ck, C_KV_HEADS), heads(cv, C_KV_HEADS), sinks)
    y_d = spatial_gating(jax.nn.gelu(du, approximate=False), jax.nn.gelu(dv, approximate=False),
                         sgu_ln_g, sgu_ln_b, sgu_w, sgu_b)
    return jnp.concatenate([y_a, y_b, y_c, y_d], axis=-1) @ w_out

def setup_inputs(seed: int = 0) -> dict:
    key = jax.random.key(seed)
    ks = jax.random.split(key, 24)
    nrm = lambda k, shape, s: jax.random.normal(k, shape, jnp.float32) * s
    L = DEPTH
    return {
        "x": nrm(ks[0], (BATCH, SEQ, D_MODEL), 1.0),
        "ln_in_g": 1.0 + nrm(ks[1], (D_MODEL,), 0.02),
        "ln_in_b": nrm(ks[2], (D_MODEL,), 0.02),
        "w_in": nrm(ks[3], (L, D_MODEL, D_IN), D_MODEL ** -0.5),
        "w_out": nrm(ks[4], (L, D_MIX, D_MODEL), D_MIX ** -0.5 * BETA),
        "pool_lin": nrm(ks[5], (L, POOL_GROUPS, POOL_CH, POOL_CH), POOL_CH ** -0.5),
        "pool_scale": 1.0 + nrm(ks[6], (L, D_GROUP), 0.1),
        "rel_bias": nrm(ks[7], (L, B_HEADS, 2 * REL_CLIP + 1), 0.3),
        "sinks": nrm(ks[8], (L, C_HEADS), 0.5),
        "sgu_ln_g": 1.0 + nrm(ks[9], (L, D_GROUP), 0.02),
        "sgu_ln_b": nrm(ks[10], (L, D_GROUP), 0.02),
        "sgu_w": nrm(ks[11], (L, SGU_GROUPS, SGU_LEN, SGU_LEN), SGU_LEN ** -0.5),
        "sgu_b": 1.0 + nrm(ks[12], (L, SGU_GROUPS, SGU_LEN), 0.01),
        "ln1_g": 1.0 + nrm(ks[13], (L, D_MODEL), 0.02),
        "ln1_b": nrm(ks[14], (L, D_MODEL), 0.02),
        "peer_wq": nrm(ks[15], (L, D_MODEL, PEER_HEADS * D_QUERY), D_MODEL ** -0.5),
        "peer_keys": nrm(ks[16], (L, PEER_HEADS, 2, N_KEYS, D_SUBKEY), D_SUBKEY ** -0.5),
        "expert_u": nrm(ks[17], (L, N_EXPERTS, D_MODEL), D_MODEL ** -0.5),
        "expert_v": nrm(ks[18], (L, N_EXPERTS, D_MODEL), BETA),
        "ln2_g": 1.0 + nrm(ks[19], (L, D_MODEL), 0.02),
        "ln2_b": nrm(ks[20], (L, D_MODEL), 0.02),
    }

def reference(x, ln_in_g, ln_in_b, w_in, w_out, pool_lin, pool_scale, rel_bias, sinks,
              sgu_ln_g, sgu_ln_b, sgu_w, sgu_b, ln1_g, ln1_b, peer_wq, peer_keys,
              expert_u, expert_v, ln2_g, ln2_b):
    x = layer_norm(x, ln_in_g, ln_in_b)
    for l in range(DEPTH):
        mix = hybrid_mixer(x, w_in[l], w_out[l], pool_lin[l], pool_scale[l], rel_bias[l], sinks[l],
                           sgu_ln_g[l], sgu_ln_b[l], sgu_w[l], sgu_b[l])
        x = layer_norm(ALPHA * x + mix, ln1_g[l], ln1_b[l])
        ffn = peer_ffn(x, peer_wq[l], peer_keys[l], expert_u[l], expert_v[l])
        x = layer_norm(ALPHA * x + ffn, ln2_g[l], ln2_b[l])
    return x


_drawn_inputs = setup_inputs


def setup_inputs(seed=0):
    import zlib

    import numpy as np

    out = dict(_drawn_inputs(seed))
    spreads = {}
    factors = {'sinks': 19.925,
     'sgu_ln_g': 16.424,
     'sgu_ln_b': 10.895,
     'sgu_b': 15.246,
     'ln2_g': 22.858,
     'ln2_b': 23.714,
     'rel_bias': 2.915}
    for name, (base, spread) in spreads.items():
        noise = np.random.default_rng([zlib.crc32(name.encode()), seed]).standard_normal(out[name].shape)
        drawn = base * np.exp(spread * noise) if base else spread * noise
        out[name] = __import__('jax').numpy.asarray(drawn.astype(out[name].dtype))
    for name, factor in factors.items():
        out[name] = (out[name] * factor).astype(out[name].dtype)
    return out
```

```python
from contextlib import ExitStack

import numpy as np
import concourse.bass as bass
from concourse import mybir

F32 = mybir.dt.float32
U32 = mybir.dt.uint32
ALU = mybir.AluOpType
ACT = mybir.ActivationFunctionType
AX = mybir.AxisListType

P = 128
T = 512
D = 1024
TB = T // P
DC = D // P
GROUP = 256
DH = 64
HEADS = 4
CHUNK = 64
POOL_WINDOWS = (2, 4, 8, 16)
REL_CLIP = 128
ALPHA = 2.0 ** 0.25
EPS = 1e-5
NEG = -1e30
SCALE = DH ** -0.5
LOWEST = -3.0e38
PH = 8
TOPK = 16
NKEYS = 128
NHZ = 2 * PH
NSEL = PH * TOPK
UN = 8
STEPS = NSEL // UN

CH_CHUNKS = 9
A0, BQ0, BK0, CQ0, CK0 = 0, 2, 4, 6, 8
TOK0 = CH_CHUNKS * P
BV0, CV0, DU0, DV0 = 0, 256, 384, 640
TOKW = 896
C_HEAD_AT = (0, 2, 1, 3)
BANKS = 8


def attention_tiles():
    tiles = []
    for h in range(HEADS):
        for qb in range(TB):
            tiles.append(("b", h, qb, list(range(qb + 1))))
            tiles.append(("c", h, qb, list(range(max(0, qb - 1), qb + 1))))
    return tiles


ATT = attention_tiles()
NATT = len(ATT)


def psum_jobs():
    jobs = []
    for tb in range(TB):
        jobs += [(("xT", tb, half), "act") for half in range(2)]
    jobs += [(("bias", i), "dve") for i in range(2)]
    for c in range(CH_CHUNKS):
        jobs.append((("hT", c), "act" if c % 2 else "dve"))
    for tb in range(TB):
        jobs += [(("vals", tb), "dve"), (("gates", tb), "act")]
    for n in range(NATT + 2):
        if n < NATT:
            jobs.append((("S", n), "dve"))
        if 1 <= n <= NATT:
            jobs.append((("PT", n - 1), "act"))
        if n >= 2:
            jobs.append((("PV", n - 2), "dve"))
    jobs += [(("pool", c), "act") for c in range(2)]
    jobs += [(("sgu", tb), "dve") for tb in range(TB)]
    jobs += [(("mixT", c), "act") for c in range(6)]
    for tb in range(TB):
        jobs += [(("out", tb, half), "dve") for half in range(2)]
    for tb in range(TB):
        jobs += [(("x1T", tb, half), "act") for half in range(2)]
    for c in range(NHZ):
        jobs.append((("q", c), "act" if c % 2 else "dve"))
    for tb in range(TB):
        jobs += [(("sc", tb, g), "dve") for g in range(4)]
    return jobs


JOBS = psum_jobs()
JOB_AT = {name: n for n, (name, _) in enumerate(JOBS)}


def evacuations(upto):
    return {e: sum(1 for _, x in JOBS[:upto] if x == e) for e in ("act", "dve")}


def hybrid_layer(nc, x, w_in, w_out, pool_lin, pool_scale, rel_ext, sinks, sgu_ln_g, sgu_ln_b, sgu_wT,
                 sgu_bT, ln_in_g, ln_in_b, ln1_g, ln1_b, ln2_g, ln2_b, peer_wq, keysT, expert_u, expert_v,
                 identity_c, flip_c, alibi_c, inv_count_c, iota_c, out):
    with ExitStack() as ctx:
        def sb(name, shape, dt=F32):
            return ctx.enter_context(nc.sbuf_tensor(name, shape, dt))

        def sem(name):
            return ctx.enter_context(nc.semaphore(name))

        arena_w = sb("arena_w", [P, DC * 2048])
        w_in_sb = arena_w[:, :].rearrange("p (c n) -> p c n", c=DC)
        wq_sb = w_in_sb
        u_ring = arena_w[:, 0:UN * D].rearrange("p (s d) -> p s d", s=UN)
        arena_o = sb("arena_o", [P, 2 * DC * D])
        w_out_sb = arena_o[:, 0:DC * D].rearrange("p (c n) -> p c n", c=DC)
        cand = arena_o[:, 0:2048]
        hot_i = arena_o[:, 2048:4096]
        hot_j = arena_o[:, 4096:6144]
        high = DC * D
        mix_tok = arena_o[:, high:high + TB * 768].rearrange("p (t n) -> p t n", t=TB)
        lnv = [arena_o[:, high + 3072 + i * D:high + 3072 + (i + 1) * D] for i in range(4)]
        alibi = arena_o[:, high + 7168:high + 8192].rearrange("p (h n) -> p h n", h=HEADS)
        qT = arena_o[:, high:high + NHZ * T].rearrange("p (c t) -> p c t", c=NHZ)
        v_ring = arena_o[:, high:high + UN * D].rearrange("p (s d) -> p s d", s=UN)

        x_sb = sb("x_sb", [P, TB, D])
        xT = sb("xT", [P, DC, T])
        mixT = xT
        ln2v = [xT[:, 4 + 2 * i:6 + 2 * i, :].rearrange("p c t -> p (c t)") for i in range(2)]
        hT = sb("hT", [P, CH_CHUNKS, T])
        x1T = hT[:, 0:DC, :]
        ht = sb("ht", [P, TB, TOKW])
        keys_sb = ht[:, :, :].rearrange("p t n -> p (t n)")[:, 0:NHZ * NKEYS]\
            .rearrange("p (c n) -> p c n", c=NHZ)
        idx_f = ht[:, :, :].rearrange("p t n -> p (t n)")[:, 2048:2048 + 4 * NSEL]\
            .rearrange("p (t n) -> p t n", t=TB)
        gate = ht[:, :, :].rearrange("p t n -> p (t n)")[:, 2560:2560 + 4 * NSEL]\
            .rearrange("p (t n) -> p t n", t=TB)

        ident = sb("ident", [P, P])
        bias_b = sb("bias_b", [P, HEADS, 256])
        s_sb = sb("s_sb", [P, 2, T])
        pT_sb = sb("pT_sb", [P, 2, T])
        flip = pT_sb[:, 0, 0:P]
        topv = s_sb[:, 0, 0:256]
        topi_f = s_sb[:, 0, 256:512]
        work = s_sb[:, 1, 0:256]
        topi = pT_sb[:, 0, 0:256].bitcast(U32)
        best = pT_sb[:, 0, 256:384]
        pos = pT_sb[:, 0, 384:512].bitcast(U32)
        pos_a = pT_sb[:, 1, 0:128].bitcast(U32)
        pos_b = pT_sb[:, 1, 128:256].bitcast(U32)
        pos_af = pT_sb[:, 1, 256:384]
        pos_bf = pT_sb[:, 1, 384:512]
        pool_lin_sb = sb("pool_lin_sb", [P, 2, DH])
        pool_scale_sb = sb("pool_scale_sb", [P, 2])
        inv_count = sb("inv_count", [P, 2, 16])
        iota16 = sb("iota16", [P, 16])
        sink_sb = sb("sink_sb", [P, HEADS])
        sgu_b_sb = sb("sgu_b_sb", [P, HEADS])
        stats = sb("stats", [P, 2, 6])
        mean_var = sb("mean_var", [P, 2])
        std = sb("std", [P, 2])
        eps = sb("eps", [P, 1])
        row = sb("row", [P, 8, 4])
        idx_stage = sb("idx_stage", [P, UN], U32)
        idx_u = sb("idx_u", [P, TB, NSEL], U32)
        hidden = sb("hidden", [P, UN])
        act_h = sb("act_h", [P, UN])
        coef = sb("coef", [P, UN])
        small = sb("small", [P, 16])
        sgu_w_sb = lnv[0][:, 0:HEADS * P].rearrange("p (g t) -> p g t", g=HEADS)
        lnv_sgu = lnv[0][:, 512:1024].rearrange("p (i n) -> p i n", i=2)

        psum = ctx.enter_context(nc.psum_tensor("psum", [P, BANKS, 512], F32))

        pair = [psum[:, 2 * i:2 * i + 2, :].rearrange("p b n -> p (b n)") for i in range(4)]
        x1_ps, acc, prod = pair[0], pair[1], pair[2:4]

        x_loaded = [sem(f"x_loaded{t}") for t in range(TB)]
        w_in_loaded = [sem(f"w_in_loaded{c}") for c in range(DC)]
        ln_in_loaded = sem("ln_in_loaded")
        tables_loaded = sem("tables_loaded")
        bias_loaded = sem("bias_loaded")
        sgu_w_loaded = sem("sgu_w_loaded")
        w_out_loaded = sem("w_out_loaded")
        wq_loaded = [sem(f"wq_loaded{c}") for c in range(DC)]
        keys_loaded = sem("keys_loaded")
        ln2_loaded = sem("ln2_loaded")
        pe_job = sem("pe_job")
        act_evac = sem("act_evac")
        dve_evac = sem("dve_evac")
        dve_chain = sem("dve_chain")
        pool_chain = sem("pool_chain")
        eps_set = sem("eps_set")
        masks_set = sem("masks_set")
        var_ready = sem("var_ready")
        std_ready = sem("std_ready")
        scaled_ready = sem("scaled_ready")
        ln_done = sem("ln_done")
        max_ready = sem("max_ready")
        exp_done = sem("exp_done")
        sink_exp_done = sem("sink_exp_done")
        pooled = sem("pooled")
        gate_in = sem("gate_in")
        gate_exp = sem("gate_exp")
        idx_ready = sem("idx_ready")
        idx_staged = sem("idx_staged")
        step_begun = sem("step_begun")
        u_loaded = [sem(f"u_loaded{s}") for s in range(UN)]
        v_loaded = [sem(f"v_loaded{s}") for s in range(UN)]
        u_free = [sem(f"u_free{s}") for s in range(UN)]
        v_free = [sem(f"v_free{s}") for s in range(UN)]
        hidden_ready = sem("hidden_ready")
        act_ready = sem("act_ready")
        y_ready = sem("y_ready")
        stored = sem("stored")

        evac_sem = {"act": act_evac, "dve": dve_evac}

        def bank(name):
            return psum[:, JOB_AT[name] % BANKS, :]

        def produced(eng, name):
            eng.wait_ge(pe_job, JOB_AT[name] + 1)

        def evacuated(eng, name):
            n = JOB_AT[name]
            e = JOBS[n][1]
            eng.wait_ge(evac_sem[e], evacuations(n + 1)[e])

        LN_IN, LN_SGU, LN_1, LN_2 = 0, 4, 8, 12
        N_TABLES = 10

        block = ctx.enter_context(nc.Block())

        @block.sync
        def _(sp):
            def bcast(dst, src, done):
                n = src.shape[0]
                sp.dma_start(dst, src.rearrange("(a n) -> a n", a=1).to_broadcast([P, n])).then_inc(done, 16)

            for tb in range(TB):
                sp.dma_start(x_sb[:, tb, :], x[tb * P:(tb + 1) * P, :]).then_inc(x_loaded[tb], 16)
                if tb == 0:
                    bcast(lnv[0], ln_in_g, ln_in_loaded)
                    bcast(lnv[1], ln_in_b, ln_in_loaded)
                    sp.dma_start(ident[:, :], identity_c).then_inc(tables_loaded, 16)
            for c in range(DC):
                sp.dma_start(w_in_sb[:, c, :], w_in[c * P:(c + 1) * P, :]).then_inc(w_in_loaded[c], 16)
            sp.dma_start(alibi, alibi_c).then_inc(tables_loaded, 16)
            sp.dma_start(pool_lin_sb[:, :, :], pool_lin).then_inc(tables_loaded, 16)
            sp.dma_start(pool_scale_sb[:, :], pool_scale).then_inc(tables_loaded, 16)
            sp.dma_start(inv_count[:, :, :], inv_count_c).then_inc(tables_loaded, 16)
            sp.dma_start(iota16[:, :], iota_c).then_inc(tables_loaded, 16)
            bcast(sink_sb[:, :], sinks, tables_loaded)
            sp.dma_start(sgu_b_sb[:, :], sgu_bT).then_inc(tables_loaded, 16)
            bcast(lnv[2], ln1_g, tables_loaded)
            bcast(lnv[3], ln1_b, tables_loaded)
            for h in range(HEADS):
                src = bass.AP(tensor=rel_ext.tensor, offset=h * 512 + 1, ap=[[1, P], [1, 256]])
                if h == 0:
                    sp.dma_start(flip, flip_c).then_inc(bias_loaded, 16)
                sp.dma_start(s_sb[:, h // 2, (h % 2) * 256:(h % 2) * 256 + 256], src).then_inc(bias_loaded, 16)
            sp.dma_start(w_out_sb, w_out.rearrange("(c p) n -> p c n", p=P)).then_inc(w_out_loaded, 16)
            sp.wait_ge(ln_done, LN_IN + TB)
            sp.dma_start(sgu_w_sb, sgu_wT).then_inc(sgu_w_loaded, 16)
            bcast(lnv_sgu[:, 0, :], sgu_ln_g, sgu_w_loaded)
            bcast(lnv_sgu[:, 1, :], sgu_ln_b, sgu_w_loaded)
            produced(sp, ("gates", TB - 1))
            for c in range(DC):
                sp.dma_start(wq_sb[:, c, :], peer_wq[c * P:(c + 1) * P, :]).then_inc(wq_loaded[c], 16)
            evacuated(sp, ("sgu", TB - 1))
            sp.dma_start(keys_sb, keysT).then_inc(keys_loaded, 16)
            produced(sp, ("out", TB - 1, 1))
            bcast(ln2v[0], ln2_g, ln2_loaded)
            bcast(ln2v[1], ln2_b, ln2_loaded)
            for tb in range(TB):
                sp.wait_ge(ln_done, LN_2 + tb + 1)
                sp.dma_start(out[tb * P:(tb + 1) * P, :], x_sb[:, tb, :]).then_inc(stored, 16)
            sp.wait_ge(stored, 16 * TB)

        @block.tensor
        def _(pe):
            opened = [0]

            def open_job(name):
                n = JOB_AT[name]
                assert n == opened[0]
                opened[0] += 1
                if n >= BANKS:
                    evacuated(pe, JOBS[n - BANKS][0])
                return bank(name)

            def close(ins):
                ins.then_inc(pe_job, 1)

            pe.wait_ge(tables_loaded, 16 * N_TABLES)
            for tb in range(TB):
                pe.wait_ge(ln_done, LN_IN + tb + 1)
                for half in range(2):
                    ps = open_job(("xT", tb, half))
                    for j in range(4):
                        c = 4 * half + j
                        last = nc.tensor.transpose(ps[:, j * P:(j + 1) * P], x_sb[:, tb, c * P:(c + 1) * P],
                                                   ident[:, :])
                    close(last)
            pe.wait_ge(bias_loaded, 16 * (HEADS + 1))
            for i in range(2):
                close(nc.tensor.matmul(open_job(("bias", i)), flip, s_sb[:, i, :], start=True, stop=True))
            evacuated(pe, ("xT", TB - 1, 1))
            for m in range(CH_CHUNKS):
                ps = open_job(("hT", m))
                for c in range(DC):
                    if m == 0:
                        pe.wait_ge(w_in_loaded[c], 16)
                    last = nc.tensor.matmul(ps[:, :], w_in_sb[:, c, m * P:(m + 1) * P], xT[:, c, :],
                                            start=(c == 0), stop=(c == DC - 1))
                close(last)
            for tb in range(TB):
                for name, col, width in (("vals", 0, 384), ("gates", 384, 512)):
                    ps = open_job((name, tb))
                    for c in range(DC):
                        last = nc.tensor.matmul(ps[:, 0:width], xT[:, c, tb * P:(tb + 1) * P],
                                                w_in_sb[:, c, TOK0 + col:TOK0 + col + width],
                                                start=(c == 0), stop=(c == DC - 1))
                    close(last)

            def scores(n):
                kind, h, qb, kbs = ATT[n]
                ps = open_job(("S", n))
                at = h if kind == "b" else C_HEAD_AT[h]
                lo = DH * (at % 2)
                qc = (BQ0 if kind == "b" else CQ0) + at // 2
                kc = BK0 + h // 2 if kind == "b" else CK0
                evacuated(pe, ("hT", qc))
                evacuated(pe, ("hT", kc))
                close(nc.tensor.matmul(ps[:, 0:P * len(kbs)], hT[lo:lo + DH, qc, qb * P:(qb + 1) * P],
                                       hT[lo:lo + DH, kc, kbs[0] * P:(kbs[-1] + 1) * P],
                                       start=True, stop=True))

            def transposes(n):
                ps = open_job(("PT", n))
                pe.wait_ge(exp_done, n + 1)
                for j in range(len(ATT[n][3])):
                    last = nc.tensor.transpose(ps[:, j * P:(j + 1) * P], s_sb[:, n % 2, j * P:(j + 1) * P],
                                               ident[:, :])
                close(last)

            def values(n):
                kind, h, qb, kbs = ATT[n]
                ps = open_job(("PV", n))
                col = BV0 + DH * h if kind == "b" else CV0 + DH * (h // 2)
                evacuated(pe, ("vals", kbs[-1]))
                evacuated(pe, ("PT", n))
                for j, kb in enumerate(kbs):
                    last = nc.tensor.matmul(ps[:, 0:DH], pT_sb[:, n % 2, j * P:(j + 1) * P],
                                            ht[:, kb, col:col + DH], start=(j == 0), stop=(j == len(kbs) - 1))
                close(last)

            for n in range(NATT + 2):
                if n < NATT:
                    scores(n)
                if 1 <= n <= NATT:
                    transposes(n - 1)
                if n >= 2:
                    values(n - 2)
            for c in range(2):
                ps = open_job(("pool", c))
                pe.wait_ge(pooled, c + 1)
                for g in range(2):
                    lo = DH * g
                    last = nc.tensor.matmul(ps[lo:lo + DH, :], pool_lin_sb[lo:lo + DH, c, :],
                                            hT[lo:lo + DH, A0 + c, :], start=True, stop=True)
                close(last)
            pe.wait_ge(masks_set, 2)
            for tb in range(TB):
                ps = open_job(("sgu", tb))
                pe.wait_ge(ln_done, LN_SGU + tb + 1)
                for g in range(HEADS):
                    last = nc.tensor.matmul(ps[:, g * DH:(g + 1) * DH], sgu_w_sb[:, g, :],
                                            ht[:, tb, DV0 + g * DH:DV0 + (g + 1) * DH], start=True, stop=True)
                close(last)
            for c in range(6):
                ps = open_job(("mixT", c))
                evacuated(pe, ("PV", NATT - 1) if c < 4 else ("sgu", TB - 1))
                for tb in range(TB):
                    last = nc.tensor.transpose(ps[:, tb * P:(tb + 1) * P], mix_tok[:, tb, c * P:(c + 1) * P],
                                               ident[:, :])
                close(last)
            pe.wait_ge(w_out_loaded, 16)
            for tb in range(TB):
                for half in range(2):
                    ps = open_job(("out", tb, half))
                    for c in range(DC):
                        evacuated(pe, ("pool", c) if c < 2 else ("mixT", c - 2))
                        last = nc.tensor.matmul(ps[:, :], mixT[:, c, tb * P:(tb + 1) * P],
                                                w_out_sb[:, c, half * 512:(half + 1) * 512],
                                                start=(c == 0), stop=(c == DC - 1))
                    close(last)
            for tb in range(TB):
                pe.wait_ge(ln_done, LN_1 + tb + 1)
                for half in range(2):
                    ps = open_job(("x1T", tb, half))
                    for j in range(4):
                        c = 4 * half + j
                        last = nc.tensor.transpose(ps[:, j * P:(j + 1) * P], x_sb[:, tb, c * P:(c + 1) * P],
                                                   ident[:, :])
                    close(last)
            evacuated(pe, ("x1T", TB - 1, 1))
            for m in range(NHZ):
                ps = open_job(("q", m))
                for c in range(DC):
                    if m == 0:
                        pe.wait_ge(wq_loaded[c], 16)
                    last = nc.tensor.matmul(ps[:, :], wq_sb[:, c, m * P:(m + 1) * P], x1T[:, c, :],
                                            start=(c == 0), stop=(c == DC - 1))
                close(last)
            pe.wait_ge(keys_loaded, 16)
            evacuated(pe, ("q", NHZ - 2))
            evacuated(pe, ("q", NHZ - 1))
            for tb in range(TB):
                for g in range(4):
                    ps = open_job(("sc", tb, g))
                    for j in range(4):
                        m = 4 * g + j
                        last = nc.tensor.matmul(ps[:, j * P:(j + 1) * P], qT[:, m, tb * P:(tb + 1) * P],
                                                keys_sb[:, m, :], start=True, stop=True)
                    close(last)

        @block.scalar
        def _(act):
            def evac(name, out_ap, in_ap, func=ACT.Copy, **kw):
                produced(act, name)
                nc.scalar.activation(out_ap, in_ap, func, **kw).then_inc(act_evac, 1)

            def ln_std(n):
                act.wait_ge(var_ready, n + 1)
                nc.scalar.activation(std[:, 0:1], mean_var[:, 1:2], ACT.Sqrt, bias=eps[:, :]).then_inc(std_ready, 1)

            act.wait_ge(eps_set, 1)
            for tb in range(TB):
                ln_std(LN_IN + tb)
            for tb in range(TB):
                for half in range(2):
                    evac(("xT", tb, half), xT[:, 4 * half:4 * half + 4, tb * P:(tb + 1) * P],
                         bank(("xT", tb, half)).rearrange("p (j t) -> p j t", j=4))
            for m in range(1, CH_CHUNKS, 2):
                evac(("hT", m), hT[:, m, :], bank(("hT", m)))
            for tb in range(TB):
                evac(("gates", tb), ht[:, tb, DU0:TOKW], bank(("gates", tb)), ACT.Gelu)
            for tb in range(TB):
                ln_std(LN_SGU + tb)
            for n in range(NATT + 1):
                if n < NATT:
                    kind, h, qb, kbs = ATT[n]
                    act.wait_ge(max_ready, n + 1)
                    s = s_sb[:, n % 2, 0:P * len(kbs)]
                    r = row[:, n % 8, :]
                    if kind == "c":
                        nc.scalar.activation(small[:, n % 8:n % 8 + 1], sink_sb[:, h:h + 1], ACT.Exp,
                                             bias=r[:, 1:2]).then_inc(sink_exp_done, 1)
                    nc.scalar.activation(s, s, ACT.Exp, bias=r[:, 1:2], accum_out=r[:, 2:3]).then_inc(exp_done, 1)
                if n >= 1:
                    m = n - 1
                    if m >= 2:
                        produced(act, ("PV", m - 2))
                    w = P * len(ATT[m][3])
                    evac(("PT", m), pT_sb[:, m % 2, 0:w], bank(("PT", m))[:, 0:w])
            for c in range(2):
                evac(("pool", c), mixT[:, c, :], bank(("pool", c)), scale=pool_scale_sb[:, c:c + 1])
            for c in range(6):
                evac(("mixT", c), mixT[:, 2 + c, :], bank(("mixT", c)))
            for tb in range(TB):
                ln_std(LN_1 + tb)
            for tb in range(TB):
                for half in range(2):
                    evac(("x1T", tb, half), x1T[:, 4 * half:4 * half + 4, tb * P:(tb + 1) * P],
                         bank(("x1T", tb, half)).rearrange("p (j t) -> p j t", j=4))
            for m in range(1, NHZ, 2):
                evac(("q", m), qT[:, m, :], bank(("q", m)))
            for tb in range(TB):
                act.wait_ge(gate_in, tb + 1)
                nc.scalar.activation(gate[:, tb, :], gate[:, tb, :], ACT.Exp).then_inc(gate_exp, 1)
            for tb in range(TB):
                with act.Fori(0, STEPS) as c:
                    act.wait_ge(hidden_ready, c + (tb * STEPS + 1))
                    nc.scalar.activation(act_h[:, :], hidden[:, :], ACT.Gelu).then_inc(act_ready, 1)
            for tb in range(TB):
                ln_std(LN_2 + tb)

        @block.vector
        def _(dve):
            steps = [0]

            def link(ins):
                steps[0] += 1
                ins.then_inc(dve_chain, 1)
                dve.wait_ge(dve_chain, steps[0])

            def evac_done(ins):
                ins.then_inc(dve_evac, 1)

            def layer_norm(n, src, width):
                pieces = max(1, width // 512)
                w = width // pieces
                for i in range(pieces):
                    last = nc.vector.bn_stats(stats[:, i, :], src[:, i * w:(i + 1) * w])
                link(last)
                nc.vector.bn_aggr(mean_var[:, :], stats[:, 0:pieces, :].rearrange("p a b -> p (a b)"))\
                    .then_inc(var_ready, 1)
                dve.wait_ge(std_ready, n + 1)
                link(nc.vector.reciprocal(std[:, 1:2], std[:, 0:1]))
                nc.vector.tensor_scalar(src, src, mean_var[:, 0:1], std[:, 1:2], ALU.subtract, ALU.mult)\
                    .then_inc(scaled_ready, 1)

            for tb in range(TB):
                dve.wait_ge(x_loaded[tb], 16)
                layer_norm(LN_IN + tb, x_sb[:, tb, :], D)
            for i in range(2):
                produced(dve, ("bias", i))
                evac_done(nc.vector.tensor_copy(bias_b[:, 2 * i:2 * i + 2, :],
                                                bank(("bias", i)).rearrange("p (h n) -> p h n", h=2)))
            for m in range(0, CH_CHUNKS, 2):
                produced(dve, ("hT", m))
                evac_done(nc.vector.tensor_copy(hT[:, m, :], bank(("hT", m))))
            for tb in range(TB):
                produced(dve, ("vals", tb))
                evac_done(nc.vector.tensor_copy(ht[:, tb, 0:384], bank(("vals", tb))[:, 0:384]))
            dve.wait_ge(tables_loaded, 16 * N_TABLES)

            for tb in range(TB):
                evacuated(dve, ("gates", tb))
                layer_norm(LN_SGU + tb, ht[:, tb, DV0:DV0 + GROUP], GROUP)

            evacuated(dve, ("hT", A0 + 1))
            for c in range(2):
                a = hT[:, A0 + c, :]
                src, hi = a, 0
                for k in range(4 if c else 2):
                    shift = 1 << k
                    lo = DH if k == (3 if c else 1) else 0
                    dst = s_sb[:, k % 2, :]
                    if lo and k:
                        nc.vector.tensor_copy(dst[0:lo, :], src[0:lo, :])
                    nc.vector.tensor_copy(dst[lo:P, 0:shift], src[lo:P, 0:shift])
                    link(nc.vector.tensor_tensor(dst[lo:P, shift:T], src[lo:P, shift:T], src[lo:P, 0:T - shift],
                                                 ALU.add))
                    src = dst
                link(nc.vector.tensor_tensor(small[:, 0:16], src[:, 0:16], inv_count[:, c, :], ALU.mult))
                link(nc.vector.tensor_tensor(small[:, 0:16], small[:, 0:16], a[:, 0:16], ALU.subtract))
                for g in range(2):
                    lo = DH * g
                    w = POOL_WINDOWS[2 * c + g]
                    last = nc.vector.scalar_tensor_tensor(out=a[lo:lo + DH, 16:T], in0=src[lo:lo + DH, 16:T],
                                                          scalar=1.0 / w, in1=a[lo:lo + DH, 16:T],
                                                          op0=ALU.mult, op1=ALU.subtract)
                link(last)
                link(nc.vector.tensor_copy(a[:, 0:16], small[:, 0:16]))
                nc.vector.tensor_copy(small[:, 0:1], small[:, 0:1]).then_inc(pooled, 1)

            dve.wait_ge(masks_set, 2)
            cs = 0
            for n in range(NATT + 2):
                if n < NATT:
                    kind, h, qb, kbs = ATT[n]
                    ps = bank(("S", n))
                    produced(dve, ("S", n))
                    if n >= 2:
                        produced(dve, ("PT", n - 2))
                    s = s_sb[:, n % 2, :]
                    r = row[:, n % 8, :]
                    near = min(2, len(kbs))
                    far = P * (len(kbs) - near)
                    bias = bias_b if kind == "b" else alibi
                    if far:
                        nc.vector.tensor_scalar(s[:, 0:far], ps[:, 0:far], SCALE, bias_b[:, h, 0:1],
                                                ALU.mult, ALU.add)
                    last = nc.vector.scalar_tensor_tensor(
                        out=s[:, far:far + P * near], in0=ps[:, far:far + P * near], scalar=SCALE,
                        in1=bias[:, h, 256 - P * near:256], op0=ALU.mult, op1=ALU.add)
                    evac_done(last)
                    dve.wait_ge(dve_evac, evacuations(JOB_AT[("S", n)] + 1)["dve"])
                    link(nc.vector.reduce_max(r[:, 0:1], s[:, 0:far + P * near], AX.X))
                    if kind == "c":
                        link(nc.vector.tensor_tensor(r[:, 0:1], r[:, 0:1], sink_sb[:, h:h + 1], ALU.max))
                    nc.vector.tensor_scalar(r[:, 1:2], r[:, 0:1], -1.0, None, ALU.mult).then_inc(max_ready, 1)
                if n >= 2:
                    m = n - 2
                    kind, h, qb, kbs = ATT[m]
                    r = row[:, m % 8, :]
                    dve.wait_ge(exp_done, m + 1)
                    if kind == "c":
                        cs += 1
                        dve.wait_ge(sink_exp_done, cs)
                        link(nc.vector.tensor_tensor(r[:, 2:3], r[:, 2:3], small[:, m % 8:m % 8 + 1], ALU.add))
                    link(nc.vector.reciprocal(r[:, 3:4], r[:, 2:3]))
                    produced(dve, ("PV", m))
                    col = (0 if kind == "b" else GROUP) + DH * h
                    evac_done(nc.vector.tensor_scalar(mix_tok[:, qb, col:col + DH], bank(("PV", m))[:, 0:DH],
                                                      r[:, 3:4], None, ALU.mult))
            for tb in range(TB):
                produced(dve, ("sgu", tb))
                for g in range(HEADS):
                    last = nc.vector.scalar_tensor_tensor(
                        out=mix_tok[:, tb, 512 + g * DH:512 + (g + 1) * DH],
                        in0=bank(("sgu", tb))[:, g * DH:(g + 1) * DH], scalar=sgu_b_sb[:, g:g + 1],
                        in1=ht[:, tb, DU0 + g * DH:DU0 + (g + 1) * DH], op0=ALU.add, op1=ALU.mult)
                evac_done(last)
            for tb in range(TB):
                for half in range(2):
                    produced(dve, ("out", tb, half))
                    cols = slice(half * 512, (half + 1) * 512)
                    evac_done(nc.vector.scalar_tensor_tensor(
                        out=x_sb[:, tb, cols], in0=x_sb[:, tb, cols], scalar=ALPHA,
                        in1=bank(("out", tb, half)), op0=ALU.mult, op1=ALU.add))
                evacuated(dve, ("out", tb, 1))
                layer_norm(LN_1 + tb, x_sb[:, tb, :], D)
            for m in range(0, NHZ, 2):
                produced(dve, ("q", m))
                if m == 0:
                    dve.wait_ge(ln_done, LN_1 + TB)
                evac_done(nc.vector.tensor_copy(qT[:, m, :], bank(("q", m))))

            def top16(values, indices, scores, scratch, evacuates=False):
                link(nc.vector.max(values[:, 0:8], scores))
                nc.vector.max_index(indices[:, 0:8], values[:, 0:8], scores)
                last = nc.vector.match_replace(scratch, values[:, 0:8], scores, LOWEST)
                if evacuates:
                    evac_done(last)
                    dve.wait_ge(dve_evac, evacuates)
                else:
                    link(last)
                link(nc.vector.max(values[:, 8:16], scratch))
                link(nc.vector.max_index(indices[:, 8:16], values[:, 8:16], scratch))

            for tb in range(TB):
                for g in range(4):
                    name = ("sc", tb, g)
                    produced(dve, name)
                    for j in range(4):
                        m = 4 * g + j
                        count = evacuations(JOB_AT[name] + 1)["dve"] if j == 3 else False
                        top16(topv[:, 16 * m:16 * m + 16], topi[:, 16 * m:16 * m + 16],
                              bank(name)[:, j * P:(j + 1) * P], work[:, 0:P], count)
                tv = topv.rearrange("p (h z k) -> p h z k", h=PH, z=2)
                tf = topi_f.rearrange("p (h z k) -> p h z k", h=PH, z=2)
                c4 = cand.rearrange("p (h a b) -> p h a b", h=PH, a=TOPK)
                link(nc.vector.tensor_copy(topi_f, topi))
                shape = [P, PH, TOPK, TOPK]
                link(nc.vector.tensor_tensor(c4, tv[:, :, 0, :].unsqueeze(3).to_broadcast(shape),
                                             tv[:, :, 1, :].unsqueeze(2).to_broadcast(shape), ALU.add))
                for h in range(PH):
                    top16(best[:, 16 * h:16 * h + 16], pos[:, 16 * h:16 * h + 16],
                          cand[:, 256 * h:256 * h + 256], work)
                nc.vector.tensor_scalar(pos_a, pos, 4, None, ALU.logical_shift_right)
                link(nc.vector.tensor_scalar(pos_b, pos, 15, None, ALU.bitwise_and))
                nc.vector.tensor_copy(pos_af, pos_a)
                link(nc.vector.tensor_copy(pos_bf, pos_b))
                for z, (hot, where) in enumerate(((hot_i, pos_af), (hot_j, pos_bf))):
                    hot4 = hot.rearrange("p (h k a) -> p h k a", h=PH, k=TOPK)
                    hot3 = hot.rearrange("p (s a) -> p s a", a=TOPK)
                    link(nc.vector.tensor_tensor(hot3, where.unsqueeze(2).to_broadcast([P, NSEL, TOPK]),
                                                 iota16[:, :].unsqueeze(1).to_broadcast([P, NSEL, TOPK]),
                                                 ALU.is_equal))
                    link(nc.vector.tensor_tensor(hot4, hot4, tf[:, :, z, :].unsqueeze(2).to_broadcast(shape),
                                                 ALU.mult))
                    link(nc.vector.tensor_reduce(where, hot3, AX.X, ALU.add))
                link(nc.vector.scalar_tensor_tensor(out=idx_f[:, tb, :], in0=pos_af, scalar=float(NKEYS), in1=pos_bf,
                                                    op0=ALU.mult, op1=ALU.add))
                nc.vector.tensor_copy(idx_u[:, tb, :], idx_f[:, tb, :]).then_inc(idx_ready, 1)
                g3 = gate[:, tb, :].rearrange("p (h k) -> p h k", h=PH)
                b3 = best.rearrange("p (h k) -> p h k", h=PH)
                nc.vector.tensor_tensor(g3, b3, b3[:, :, 0:1].to_broadcast([P, PH, TOPK]), ALU.subtract)\
                    .then_inc(gate_in, 1)
                dve.wait_ge(gate_exp, tb + 1)
                link(nc.vector.tensor_reduce(small[:, 0:PH], g3, AX.X, ALU.add))
                link(nc.vector.reciprocal(small[:, 8:8 + PH], small[:, 0:PH]))
                link(nc.vector.tensor_tensor(g3, g3, small[:, 8:8 + PH].unsqueeze(2).to_broadcast([P, PH, TOPK]),
                                             ALU.mult))

            for s in range(UN):
                nc.vector.memset(hidden[:, s:s + 1], 0.0).then_inc(u_free[s], 1)
                nc.vector.memset(coef[:, s:s + 1], 0.0).then_inc(v_free[s], 1)
            done = steps[0]

            def dot(s, seq):
                dve.wait_ge(u_loaded[s], seq * 16)
                dve.wait_ge(u_free[(s - 2) % UN], seq + (1 if s >= 2 else 0))
                nc.vector.tensor_tensor_reduce(out=prod[s % 2], in0=u_ring[:, s, :], in1=x1_ps, scale=1.0, scalar=0.0,
                                               op0=ALU.mult, op1=ALU.add, accum_out=hidden[:, s:s + 1])\
                    .then_inc(u_free[s], 1)

            def add_row(s, seq):
                dve.wait_ge(v_loaded[s], seq * 16)
                dve.wait_ge(v_free[(s - 1) % UN], seq + (1 if s else 0))
                nc.vector.scalar_tensor_tensor(out=acc, in0=v_ring[:, s, :], scalar=coef[:, s:s + 1], in1=acc,
                                               op0=ALU.mult, op1=ALU.add).then_inc(v_free[s], 1)

            def coefs(tb, seq, c):
                dve.wait_ge(u_free[UN - 1], seq + 1)
                nc.vector.tensor_copy(small[:, 0:1], small[:, 0:1]).then_inc(hidden_ready, 1)
                dve.wait_ge(act_ready, seq)
                dve.wait_ge(dve_chain, chain_at(seq) - 1)
                nc.vector.tensor_tensor(coef[:, :], act_h[:, :], gate[:, tb, bass.ds(c * UN, UN)], ALU.mult)\
                    .then_inc(dve_chain, 1)
                dve.wait_ge(dve_chain, chain_at(seq))

            extra = [0]

            def chain_at(seq):
                return seq + (steps[0] - (extra[0]))

            for tb in range(TB):
                x1 = x_sb[:, tb, :]
                nc.vector.tensor_copy(x1_ps, x1)
                link(nc.vector.tensor_scalar(acc, x1, ALPHA, None, ALU.mult))
                first = tb * STEPS
                for s in range(UN):
                    dot(s, first + 1)
                extra[0] = first
                coefs(tb, first + 1, 0)
                with dve.Fori(1, STEPS) as c:
                    for s in range(UN):
                        dot(s, c + (first + 1))
                        add_row(s, c + first)
                    dve.wait_ge(v_free[UN - 1], c + (first + 1))
                    coefs(tb, c + (first + 1), c)
                for s in range(UN):
                    add_row(s, first + STEPS)
                steps[0] += STEPS
                extra[0] = first + STEPS
                dve.wait_ge(v_free[UN - 1], first + STEPS + 1)
                nc.vector.tensor_copy(x1, acc).then_inc(y_ready, 1)
                dve.wait_ge(y_ready, tb + 1)
            for tb in range(TB):
                layer_norm(LN_2 + tb, x_sb[:, tb, :], D)

        @block.gpsimd
        def _(pool):
            steps = [0]

            def link(ins):
                steps[0] += 1
                ins.then_inc(pool_chain, 1)
                pool.wait_ge(pool_chain, steps[0])

            def gain_bias(n, src, g, b):
                pool.wait_ge(scaled_ready, n + 1)
                link(nc.gpsimd.tensor_tensor(src, src, g, ALU.mult))
                nc.gpsimd.tensor_tensor(src, src, b, ALU.add).then_inc(ln_done, 1)

            nc.gpsimd.memset(eps[:, :], EPS).then_inc(eps_set, 1)
            pool.wait_ge(ln_in_loaded, 32)
            for tb in range(TB):
                gain_bias(LN_IN + tb, x_sb[:, tb, :], lnv[0], lnv[1])
            pool.wait_ge(sgu_w_loaded, 48)
            nc.gpsimd.affine_select(out=sgu_w_sb, in_=sgu_w_sb, compare_op=ALU.is_ge, fill=0.0,
                                    base=0, pattern=[[0, HEADS], [1, P]], channel_multiplier=-1)\
                .then_inc(masks_set, 1)
            evacuated(pool, ("bias", 1))
            nc.gpsimd.memset(bias_b[0:CHUNK, :, 256 - CHUNK:256], NEG).then_inc(masks_set, 1)
            pool.wait_ge(tables_loaded, 16 * N_TABLES)
            for tb in range(TB):
                gain_bias(LN_SGU + tb, ht[:, tb, DV0:DV0 + GROUP], lnv_sgu[:, 0, :], lnv_sgu[:, 1, :])
            for tb in range(TB):
                gain_bias(LN_1 + tb, x_sb[:, tb, :], lnv[2], lnv[3])

            produced(pool, ("sc", TB - 1, 3))
            for tb in range(TB):
                pool.wait_ge(idx_ready, tb + 1)
                first = tb * STEPS
                with pool.Fori(0, STEPS) as c:
                    nc.gpsimd.tensor_copy(idx_stage[:, :], idx_u[:, tb, bass.ds(c * UN, UN)]).then_inc(idx_staged, 1)
                    turn = pool.snap(c + (first + 1))
                    pool.wait_ge(idx_staged, turn)
                    pool.sem_inc(step_begun, 1)
                    for s in range(UN):
                        for ring, free, table, loaded in ((u_ring, u_free[s], expert_u, u_loaded[s]),
                                                          (v_ring, v_free[s], expert_v, v_loaded[s])):
                            pool.wait_ge(idx_ready, tb + 1)
                            pool.wait_ge(free, turn)
                            nc.gpsimd.indirect_dma_start(
                                out=ring[:, s, :], out_offset=None, in_=table,
                                in_offset=bass.IndirectOffsetOnAxis(ap=idx_stage[:, s:s + 1], axis=0))\
                                .then_inc(loaded, 16)
                    for s in range(UN):
                        pool.wait_ge(v_loaded[s], (c + (first + 1)) * 16)
            pool.wait_ge(ln2_loaded, 32)
            for tb in range(TB):
                gain_bias(LN_2 + tb, x_sb[:, tb, :], ln2v[0], ln2v[1])


def shape_constants():
    i = np.arange(P)[:, None]
    u = np.arange(2 * P)[None, :]
    dist = np.abs(P + i - u).astype(np.float32)
    key_chunk = u // CHUNK
    own = 2 + i // CHUNK
    seen = (key_chunk == own) | (key_chunk == own - 1)
    slopes = 2.0 ** (-8.0 * (np.arange(HEADS, dtype=np.float32) + 1.0) / HEADS)
    alibi = np.where(seen[:, None, :], -slopes[None, :, None] * dist[:, None, :], NEG).astype(np.float32)
    inv = np.zeros((P, 2, 16), np.float32)
    for g, w in enumerate(POOL_WINDOWS):
        inv[DH * (g % 2):DH * (g % 2) + DH, g // 2, :] = 1.0 / np.minimum(np.arange(16) + 1, w)
    iota = np.tile(np.arange(16, dtype=np.float32), (P, 1))
    return np.eye(P, dtype=np.float32), alibi, inv, iota


def kernel(**inputs):
    import concourse.bacc as bacc
    from concourse.bass_utils import run_bass_kernel_spmd

    a = {k: np.asarray(v) for k, v in inputs.items()}
    w_in = a["w_in"][0]
    cq = [1024 + DH * h + np.arange(DH) for h in C_HEAD_AT]
    order = np.concatenate([np.arange(0, 768), *cq, np.arange(1280, 1408),
                            np.arange(768, 1024), np.arange(1408, 1536), np.arange(1536, 2048)])
    rel_at = np.clip(256 - np.arange(512), -REL_CLIP, REL_CLIP) + REL_CLIP
    ident, alibi, inv, iota = shape_constants()
    arrays = {
        "x": a["x"].reshape(T, D),
        "w_in": w_in[:, order],
        "w_out": a["w_out"][0],
        "pool_lin": a["pool_lin"][0].reshape(2, 2, DH, DH).transpose(1, 2, 0, 3).reshape(P, 2, DH),
        "pool_scale": a["pool_scale"][0].reshape(2, P).T,
        "rel_ext": a["rel_bias"][0][:, rel_at],
        "sinks": a["sinks"][0],
        "sgu_ln_g": a["sgu_ln_g"][0],
        "sgu_ln_b": a["sgu_ln_b"][0],
        "sgu_wT": a["sgu_w"][0].transpose(2, 0, 1),
        "sgu_bT": a["sgu_b"][0].T,
        "ln_in_g": a["ln_in_g"], "ln_in_b": a["ln_in_b"],
        "ln1_g": a["ln1_g"][0], "ln1_b": a["ln1_b"][0],
        "ln2_g": a["ln2_g"][0], "ln2_b": a["ln2_b"][0],
        "peer_wq": a["peer_wq"][0],
        "keysT": a["peer_keys"][0].reshape(NHZ, NKEYS, P).transpose(2, 0, 1),
        "expert_u": a["expert_u"][0],
        "expert_v": a["expert_v"][0],
        "identity_c": ident, "flip_c": ident[::-1], "alibi_c": alibi, "inv_count_c": inv, "iota_c": iota,
    }
    nc = bacc.Bacc("TRN2", target_bir_lowering=False, num_devices=1)
    arrays = {f"in_{k}": np.ascontiguousarray(v) for k, v in arrays.items()}
    args = [nc.dram_tensor(k, v.shape, mybir.dt.from_np(v.dtype), kind="ExternalInput").ap()
            for k, v in arrays.items()]
    out = nc.dram_tensor("out", (T, D), F32, kind="ExternalOutput").ap()
    hybrid_layer(nc, *args, out)
    r = run_bass_kernel_spmd(nc, [arrays], core_ids=[0])
    return r.results[0]["out"].reshape(1, T, D)
```

```python
from contextlib import ExitStack

import numpy as np
import concourse.bass as bass
from concourse import mybir

F32 = mybir.dt.float32
F32R = mybir.dt.float32r
BF16 = mybir.dt.bfloat16
U32 = mybir.dt.uint32
ALU = mybir.AluOpType
ACT = mybir.ActivationFunctionType
AX = mybir.AxisListType

P = 128
T = 512
D = 1024
TB = T // P
DC = D // P
GROUP = 256
DH = 64
HEADS = 4
CHUNK = 64
POOL_WINDOWS = (2, 4, 8, 16)
REL_CLIP = 128
ALPHA = 2.0 ** 0.25
EPS = 1e-5
NEG = -1e30
SCALE = DH ** -0.5
LOWEST = -3.0e38
PH = 8
TOPK = 16
NKEYS = 128
NHZ = 2 * PH
NSEL = PH * TOPK
TOKENS = 8
WSTEPS = P // TOKENS
TILES = NKEYS
UNROLL = 4
STEPS = TILES // UNROLL
GROUP_JOBS = 2 * TB

CH_CHUNKS = 9
A0, BQ0, BK0, CQ0, CK0 = 0, 2, 4, 6, 8
TOK0 = CH_CHUNKS * P
BV0, CV0, DU0, DV0 = 0, 256, 384, 640
TOKW = 896
C_HEAD_AT = (0, 2, 1, 3)
BANKS = 6
WQ_SLOTS = 3


def attention_tiles():
    tiles = []
    for h in range(HEADS):
        for qb in range(TB):
            tiles.append(("b", h, qb, list(range(qb + 1))))
            tiles.append(("c", h, qb, list(range(max(0, qb - 1), qb + 1))))
    return tiles


ATT = attention_tiles()
NATT = len(ATT)


def psum_jobs():
    jobs = []
    for tb in range(TB):
        jobs += [(("xT", tb, half), "act") for half in range(2)]
    jobs += [(("bias", i), "dve") for i in range(2)]
    for c in range(CH_CHUNKS):
        jobs.append((("hT", c), "act" if c % 2 else "dve"))
    for tb in range(TB):
        jobs += [(("vals", tb), "dve"), (("gates", tb), "act")]
    for n in range(NATT + 2):
        if n < NATT:
            jobs.append((("S", n), "dve"))
        if 1 <= n <= NATT:
            jobs.append((("PT", n - 1), "act"))
        if n >= 2:
            jobs.append((("PV", n - 2), "dve"))
        if n < NATT:
            jobs.append((("M", n // 2, n % 2), "act" if n % 2 else "dve"))
    jobs += [(("pool", c), "act") for c in range(2)]
    jobs += [(("sgu", tb), "dve") for tb in range(TB)]
    jobs += [(("mixT", c), "act") for c in range(6)]
    for tb in range(TB):
        jobs += [(("out", tb, half), "dve") for half in range(2)]
    for tb in range(TB + 1):
        if tb < TB:
            jobs += [(("x1T", tb, half), "act") for half in range(2)]
            jobs += [(("sc", tb, g), "dve") for g in range(4)]
        if tb:
            jobs.append((("slots", tb - 1), "act"))
    return jobs


JOBS = psum_jobs()
JOB_AT = {name: n for n, (name, _) in enumerate(JOBS)}


def need(eng, semaphore, value):
    if not isinstance(value, int) or value > 0:
        eng.wait_ge(semaphore, value)


def evacuations(upto):
    return {e: sum(1 for _, x in JOBS[:upto] if x == e) for e in ("act", "dve")}


def hybrid_layer(nc, x, w_in, w_out, pool_lin, pool_scale, rel_ext, sinks, sgu_ln_g, sgu_ln_b, sgu_wT,
                 sgu_bT, ln_in_g, ln_in_b, ln1_g, ln1_b, ln2_g, ln2_b, wq_keys, expert_uT, expert_v,
                 identity_c, flip_c, alibi_c, inv_count_c, iota_c, w_dram, out):
    with ExitStack() as ctx:
        def sb(name, shape, dt=F32):
            return ctx.enter_context(nc.sbuf_tensor(name, shape, dt))

        def sem(name):
            return ctx.enter_context(nc.semaphore(name))

        x_sb = sb("x_sb", [P, TB, D])
        ident = sb("ident", [P, P])
        iota = sb("iota", [P, P])
        stats = sb("stats", [P, 2, 6])
        mean_var = sb("mean_var", [P, 2])
        std = sb("std", [P, 2])
        eps = sb("eps", [P, 1])
        row = sb("row", [P, 8, 4])
        small = sb("small", [P, 16])
        pool_lin_sb = sb("pool_lin_sb", [P, 2, DH])
        pool_scale_sb = sb("pool_scale_sb", [P, 2])
        inv_count = sb("inv_count", [P, 2, 16])
        sink_sb = sb("sink_sb", [P, HEADS])
        sgu_b_sb = sb("sgu_b_sb", [P, HEADS])

        with ExitStack() as low:
            arena_w = low.enter_context(nc.sbuf_tensor("arena_w", [P, DC * 2048], F32))
            w_in_sb = arena_w[:, :].rearrange("p (c n) -> p c n", c=DC)
            score_w = w_in_sb
            with ExitStack() as front:
                def fb(name, shape, dt=F32):
                    return front.enter_context(nc.sbuf_tensor(name, shape, dt))

                w_out_sb = fb("w_out_sb", [P, DC, D])
                mix_tok = fb("mix_tok", [P, TB, 2 * GROUP])
                ln_vectors = fb("ln_vectors", [P, 4, D])
                lnv = [ln_vectors[:, i, :] for i in range(4)]
                alibi = fb("alibi", [P, HEADS, 256])
                xT = fb("xT", [P, DC, T])
                hT = fb("hT", [P, CH_CHUNKS, T])
                ht = fb("ht", [P, TB, TOKW])
                bias_b = fb("bias_b", [P, HEADS, 256])
                s_sb = fb("s_sb", [P, 2, T])
                pT_sb = fb("pT_sb", [P, 2, T])
            mixT = xT
            wq_ring = xT[:, :, :].rearrange("p c t -> p (c t)")[:, 0:WQ_SLOTS * (D + NKEYS)]\
                .rearrange("p (s n) -> p s n", s=WQ_SLOTS)
            flip = pT_sb[:, 0, 0:P]
            sgu_w_sb = lnv[0][:, 0:HEADS * P].rearrange("p (g t) -> p g t", g=HEADS)
            lnv_sgu = lnv[0][:, 512:1024].rearrange("p (i n) -> p i n", i=2)

            with ExitStack() as route:
                def rb(name, shape, dt=F32):
                    return route.enter_context(nc.sbuf_tensor(name, shape, dt))

                rb("x_halves", [P, 2, DC, T])
                wbuf = rb("wbuf", [P, TILES, P])
                x1T = rb("x1T", [P, DC, P])
                cand = rb("cand", [P, PH * TOPK * TOPK])
                topv_t = rb("topv_t", [P, NHZ * TOPK])
                topi_t = rb("topi_t", [P, NHZ * TOPK], U32)
                topi_ft = rb("topi_ft", [P, NHZ * TOPK])
                work_t = rb("work_t", [P, TOPK * TOPK])
                best_t = rb("best_t", [P, NSEL])
                pos_t = rb("pos_t", [P, 3, NSEL], U32)
                slots = rb("slots", [P, 3, NSEL])
                slotT = rb("slotT", [P, 3, P])
                l_ring = rb("l_ring", [P, TOKENS, P])
                r_ring = rb("r_ring", [P, TOKENS, P])
                staged = rb("staged", [P, 2, TOKENS])
            topv, topi, topi_f, work = topv_t[:, :], topi_t[:, :], topi_ft[:, :], work_t[:, :]
            hot = cand[:, 0:PH * TOPK * TOPK]
            best = best_t[:, :]
            pos, pos_a, pos_b = (pos_t[:, i, :] for i in range(3))

            with ExitStack() as dense:
                def db(name, shape, dt=F32):
                    return dense.enter_context(nc.sbuf_tensor(name, shape, dt))

                x_hi = db("x_hi", [P, DC, T], F32R)
                x_lo = db("x_lo", [P, DC, T], F32R)
                a_hi = db("a_hi", [P, UNROLL, T], F32R)
                a_lo = db("a_lo", [P, UNROLL, T], F32R)
                w_tile = db("w_tile", [P, UNROLL, T])
                gelu_h = db("gelu_h", [P, 2, T])
                a_full = db("a_full", [P, 2, T])
                ln2_vectors = db("ln2_vectors", [P, 2, D])
        with ExitStack() as low:
            def eb(name, shape, dt=F32):
                return low.enter_context(nc.sbuf_tensor(name, shape, dt))

            u_raw = eb("u_raw", [P, 2, DC, P])
            v_raw = eb("v_raw", [P, 2, D])
            u_hi = eb("u_hi", [P, 2, DC, P], F32R)
            u_lo = eb("u_lo", [P, 2, DC, P], F32R)
            v_hi = eb("v_hi", [P, UNROLL, D], F32R)
            v_lo = eb("v_lo", [P, UNROLL, D], F32R)

        psum = ctx.enter_context(nc.psum_tensor("psum", [P, 8, 512], F32))

        x_loaded = [sem(f"x_loaded{t}") for t in range(TB)]
        w_in_loaded = [sem(f"w_in_loaded{c}") for c in range(DC)]
        ln_in_loaded = sem("ln_in_loaded")
        tables_loaded = sem("tables_loaded")
        bias_loaded = sem("bias_loaded")
        sgu_w_loaded = sem("sgu_w_loaded")
        w_out_loaded = sem("w_out_loaded")
        wq_loaded = [sem(f"wq_loaded{s}") for s in range(WQ_SLOTS)]
        ln2_loaded = sem("ln2_loaded")
        pe_job = sem("pe_job")
        act_evac = sem("act_evac")
        dve_evac = sem("dve_evac")
        dve_chain = sem("dve_chain")
        pool_chain = sem("pool_chain")
        eps_set = sem("eps_set")
        masks_set = sem("masks_set")
        var_ready = sem("var_ready")
        std_ready = sem("std_ready")
        scaled_ready = sem("scaled_ready")
        ln_done = sem("ln_done")
        max_ready = sem("max_ready")
        exp_done = sem("exp_done")
        sink_exp_done = sem("sink_exp_done")
        pooled = sem("pooled")
        gate_in = sem("gate_in")
        gate_exp = sem("gate_exp")
        slots_ready = sem("slots_ready")
        x_hi_done = sem("x_hi_done")
        x_lo_done = sem("x_lo_done")
        slots_staged = sem("slots_staged")
        l_built = sem("l_built")
        r_built = sem("r_built")
        w_product = sem("w_product")
        w_evac = sem("w_evac")
        pool_turn = sem("pool_turn")
        w_turn = sem("w_turn")
        w_stored = sem("w_stored")
        u_raw_loaded = [sem(f"u_raw_loaded{s}") for s in range(2)]
        v_raw_loaded = [sem(f"v_raw_loaded{s}") for s in range(2)]
        w_tile_loaded = [sem(f"w_tile_loaded{s}") for s in range(UNROLL)]
        u_hi_done = sem("u_hi_done")
        u_lo_done = sem("u_lo_done")
        v_hi_done = sem("v_hi_done")
        v_lo_done = sem("v_lo_done")
        h_done = sem("h_done")
        gelu_done = sem("gelu_done")
        a_done = sem("a_done")
        a_hi_done = sem("a_hi_done")
        a_lo_done = sem("a_lo_done")
        y_done = sem("y_done")
        y_evac = sem("y_evac")
        stored = sem("stored")

        evac_sem = {"act": act_evac, "dve": dve_evac}

        def bank(name):
            return psum[:, JOB_AT[name] % BANKS, :]

        def produced(eng, name):
            eng.wait_ge(pe_job, JOB_AT[name] + 1)

        def evacuated(eng, name):
            n = JOB_AT[name]
            e = JOBS[n][1]
            eng.wait_ge(evac_sem[e], evacuations(n + 1)[e])

        LN_IN, LN_SGU, LN_1, LN_2 = 0, 4, 8, 12
        N_TABLES = 10

        block = ctx.enter_context(nc.Block())

        @block.sync
        def _(sp):
            def bcast(dst, src, done):
                n = src.shape[0]
                sp.dma_start(dst, src.rearrange("(a n) -> a n", a=1).to_broadcast([P, n])).then_inc(done, 16)

            for tb in range(TB):
                sp.dma_start(x_sb[:, tb, :], x[tb * P:(tb + 1) * P, :]).then_inc(x_loaded[tb], 16)
                if tb == 0:
                    bcast(lnv[0], ln_in_g, ln_in_loaded)
                    bcast(lnv[1], ln_in_b, ln_in_loaded)
                    sp.dma_start(ident[:, :], identity_c).then_inc(tables_loaded, 16)
            for c in range(DC):
                sp.dma_start(w_in_sb[:, c, :], w_in[c * P:(c + 1) * P, :]).then_inc(w_in_loaded[c], 16)
            sp.dma_start(alibi[:, :, :], alibi_c).then_inc(tables_loaded, 16)
            sp.dma_start(pool_lin_sb[:, :, :], pool_lin).then_inc(tables_loaded, 16)
            sp.dma_start(pool_scale_sb[:, :], pool_scale).then_inc(tables_loaded, 16)
            sp.dma_start(inv_count[:, :, :], inv_count_c).then_inc(tables_loaded, 16)
            sp.dma_start(iota[:, :], iota_c).then_inc(tables_loaded, 16)
            bcast(sink_sb[:, :], sinks, tables_loaded)
            sp.dma_start(sgu_b_sb[:, :], sgu_bT).then_inc(tables_loaded, 16)
            bcast(lnv[2], ln1_g, tables_loaded)
            bcast(lnv[3], ln1_b, tables_loaded)
            for h in range(HEADS):
                src = bass.AP(tensor=rel_ext.tensor, offset=h * 512 + 1, ap=[[1, P], [1, 256]])
                if h == 0:
                    sp.dma_start(flip, flip_c).then_inc(bias_loaded, 16)
                sp.dma_start(s_sb[:, h // 2, (h % 2) * 256:(h % 2) * 256 + 256], src).then_inc(bias_loaded, 16)
            sp.dma_start(w_out_sb[:, :, :], w_out.rearrange("(c p) n -> p c n", p=P)).then_inc(w_out_loaded, 16)
            sp.wait_ge(ln_done, LN_IN + TB)
            sp.dma_start(sgu_w_sb, sgu_wT).then_inc(sgu_w_loaded, 16)
            bcast(lnv_sgu[:, 0, :], sgu_ln_g, sgu_w_loaded)
            bcast(lnv_sgu[:, 1, :], sgu_ln_b, sgu_w_loaded)
            produced(sp, ("gates", TB - 1))
            for m in range(NHZ):
                if m >= WQ_SLOTS:
                    produced(sp, ("M", m - WQ_SLOTS, 1))
                sp.dma_start(wq_ring[:, m % WQ_SLOTS, :], wq_keys[m]).then_inc(wq_loaded[m % WQ_SLOTS], 16)
            w_view = w_dram.rearrange("i j t -> j i t")
            for tb in range(TB):
                sp.wait_ge(w_evac, 2 + 2 * WSTEPS * (tb + 1))
                for q in range(8):
                    tiles = slice(q * TILES // 8, (q + 1) * TILES // 8)
                    sp.dma_start(w_view[:, tiles, tb * P:(tb + 1) * P], wbuf[:, tiles, :]).then_inc(w_stored, 16)
            def tile_loads(c):
                for k in range(UNROLL):
                    n = c * UNROLL + k
                    turn = c * 2 + k // 2
                    need(sp, u_lo_done, n - 1)
                    sp.dma_start(u_raw[:, k % 2, :, :].rearrange("p c e -> p (c e)"),
                                 expert_uT[bass.ds(n * P, P), :]).then_inc(u_raw_loaded[k % 2], 16)
                    need(sp, v_lo_done, n - 1)
                    sp.dma_start(v_raw[:, k % 2, :], expert_v[bass.ds(n * P, P), :])\
                        .then_inc(v_raw_loaded[k % 2], 16)
                    if isinstance(n, int) and n == 0:
                        sp.wait_ge(w_stored, 16 * 8 * TB)
                    need(sp, a_done, n - UNROLL + 1)
                    sp.dma_start(w_tile[:, k, :], w_rows[bass.ds(n * P, P), :])\
                        .then_inc(w_tile_loaded[k], 16)

            w_rows = w_dram.rearrange("i j t -> (i j) t")
            tile_loads(0)
            bcast(ln2_vectors[:, 0, :], ln2_g, ln2_loaded)
            bcast(ln2_vectors[:, 1, :], ln2_b, ln2_loaded)
            with sp.Fori(1, STEPS) as c:
                tile_loads(c)
            for tb in range(TB):
                sp.wait_ge(ln_done, LN_2 + tb + 1)
                sp.dma_start(out[tb * P:(tb + 1) * P, :], x_sb[:, tb, :]).then_inc(stored, 16)
            sp.wait_ge(stored, 16 * TB)

        @block.tensor
        def _(pe):
            opened = [0]

            def open_job(name):
                n = JOB_AT[name]
                assert n == opened[0]
                opened[0] += 1
                if n >= BANKS:
                    evacuated(pe, JOBS[n - BANKS][0])
                return bank(name)

            def close(ins):
                ins.then_inc(pe_job, 1)

            pe.wait_ge(tables_loaded, 16 * N_TABLES)
            for tb in range(TB):
                pe.wait_ge(ln_done, LN_IN + tb + 1)
                for half in range(2):
                    ps = open_job(("xT", tb, half))
                    for j in range(4):
                        c = 4 * half + j
                        last = nc.tensor.transpose(ps[:, j * P:(j + 1) * P], x_sb[:, tb, c * P:(c + 1) * P],
                                                   ident[:, :])
                    close(last)
            pe.wait_ge(bias_loaded, 16 * (HEADS + 1))
            for i in range(2):
                close(nc.tensor.matmul(open_job(("bias", i)), flip, s_sb[:, i, :], start=True, stop=True))
            evacuated(pe, ("xT", TB - 1, 1))
            for m in range(CH_CHUNKS):
                ps = open_job(("hT", m))
                for c in range(DC):
                    if m == 0:
                        pe.wait_ge(w_in_loaded[c], 16)
                    last = nc.tensor.matmul(ps[:, :], w_in_sb[:, c, m * P:(m + 1) * P], xT[:, c, :],
                                            start=(c == 0), stop=(c == DC - 1))
                close(last)
            for tb in range(TB):
                for name, col, width in (("vals", 0, 384), ("gates", 384, 512)):
                    ps = open_job((name, tb))
                    for c in range(DC):
                        last = nc.tensor.matmul(ps[:, 0:width], xT[:, c, tb * P:(tb + 1) * P],
                                                w_in_sb[:, c, TOK0 + col:TOK0 + col + width],
                                                start=(c == 0), stop=(c == DC - 1))
                    close(last)

            def scores(n):
                kind, h, qb, kbs = ATT[n]
                ps = open_job(("S", n))
                at = h if kind == "b" else C_HEAD_AT[h]
                lo = DH * (at % 2)
                qc = (BQ0 if kind == "b" else CQ0) + at // 2
                kc = BK0 + h // 2 if kind == "b" else CK0
                evacuated(pe, ("hT", qc))
                evacuated(pe, ("hT", kc))
                close(nc.tensor.matmul(ps[:, 0:P * len(kbs)], hT[lo:lo + DH, qc, qb * P:(qb + 1) * P],
                                       hT[lo:lo + DH, kc, kbs[0] * P:(kbs[-1] + 1) * P],
                                       start=True, stop=True))

            def transposes(n):
                ps = open_job(("PT", n))
                pe.wait_ge(exp_done, n + 1)
                for j in range(len(ATT[n][3])):
                    last = nc.tensor.transpose(ps[:, j * P:(j + 1) * P], s_sb[:, n % 2, j * P:(j + 1) * P],
                                               ident[:, :])
                close(last)

            def values(n):
                kind, h, qb, kbs = ATT[n]
                ps = open_job(("PV", n))
                col = BV0 + DH * h if kind == "b" else CV0 + DH * (h // 2)
                evacuated(pe, ("vals", kbs[-1]))
                evacuated(pe, ("PT", n))
                for j, kb in enumerate(kbs):
                    last = nc.tensor.matmul(ps[:, 0:DH], pT_sb[:, n % 2, j * P:(j + 1) * P],
                                            ht[:, kb, col:col + DH], start=(j == 0), stop=(j == len(kbs) - 1))
                close(last)

            def fold(m, g):
                ps = open_job(("M", m, g))
                pe.wait_ge(wq_loaded[m % WQ_SLOTS], 16 * (m // WQ_SLOTS + 1))
                for j in range(4):
                    c = 4 * g + j
                    last = nc.tensor.matmul(ps[:, j * P:(j + 1) * P], wq_ring[:, m % WQ_SLOTS, c * P:(c + 1) * P],
                                            wq_ring[:, m % WQ_SLOTS, D:D + NKEYS], start=True, stop=True)
                close(last)

            for n in range(NATT + 2):
                if n < NATT:
                    scores(n)
                if 1 <= n <= NATT:
                    transposes(n - 1)
                if n >= 2:
                    values(n - 2)
                if n < NATT:
                    fold(n // 2, n % 2)
            for c in range(2):
                ps = open_job(("pool", c))
                pe.wait_ge(pooled, c + 1)
                for g in range(2):
                    lo = DH * g
                    last = nc.tensor.matmul(ps[lo:lo + DH, :], pool_lin_sb[lo:lo + DH, c, :],
                                            hT[lo:lo + DH, A0 + c, :], start=True, stop=True)
                close(last)
            pe.wait_ge(masks_set, 2)
            for tb in range(TB):
                ps = open_job(("sgu", tb))
                pe.wait_ge(ln_done, LN_SGU + tb + 1)
                for g in range(HEADS):
                    last = nc.tensor.matmul(ps[:, g * DH:(g + 1) * DH], sgu_w_sb[:, g, :],
                                            ht[:, tb, DV0 + g * DH:DV0 + (g + 1) * DH], start=True, stop=True)
                close(last)
            for c in range(6):
                ps = open_job(("mixT", c))
                evacuated(pe, ("PV", NATT - 1) if c < 4 else ("sgu", TB - 1))
                for tb in range(TB):
                    src = mix_tok[:, tb, c * P:(c + 1) * P] if c < 4 else \
                        ht[:, tb, DU0 + (c - 4) * P:DU0 + (c - 3) * P]
                    last = nc.tensor.transpose(ps[:, tb * P:(tb + 1) * P], src, ident[:, :])
                close(last)
            pe.wait_ge(w_out_loaded, 16)
            for tb in range(TB):
                for half in range(2):
                    ps = open_job(("out", tb, half))
                    for c in range(DC):
                        evacuated(pe, ("pool", c) if c < 2 else ("mixT", c - 2))
                        last = nc.tensor.matmul(ps[:, :], mixT[:, c, tb * P:(tb + 1) * P],
                                                w_out_sb[:, c, half * 512:(half + 1) * 512],
                                                start=(c == 0), stop=(c == DC - 1))
                    close(last)
            pe.sem_inc(w_product, 2)
            for tb in range(TB + 1):
                if tb < TB:
                    pe.wait_ge(ln_done, LN_1 + tb + 1)
                    for half in range(2):
                        ps = open_job(("x1T", tb, half))
                        for j in range(4):
                            c = 4 * half + j
                            last = nc.tensor.transpose(ps[:, j * P:(j + 1) * P],
                                                       x_sb[:, tb, c * P:(c + 1) * P], ident[:, :])
                        close(last)
                    evacuated(pe, ("x1T", tb, 1))
                    for g in range(4):
                        ps = open_job(("sc", tb, g))
                        evacuated(pe, ("M", NHZ - 1, 0))
                        evacuated(pe, ("M", NHZ - 1, 1))
                        for c in range(DC):
                            last = nc.tensor.matmul(ps[:, :], x1T[:, c, :], score_w[:, c, g * 512:(g + 1) * 512],
                                                    start=(c == 0), stop=(c == DC - 1))
                        close(last)
                if tb:
                    b = tb - 1
                    pe.wait_ge(slots_ready, b + 1)
                    ps = open_job(("slots", b))
                    for i in range(3):
                        last = nc.tensor.transpose(ps[:, i * P:(i + 1) * P], slots[:, i, :], ident[:, :])
                    close(last)
                    with pe.Fori(0, WSTEPS) as g:
                        for half in range(2):
                            done = (g + b * WSTEPS) * 2 + half
                            pe.wait_ge(l_built, (done + 1) * (TOKENS // 2) + 1)
                            pe.wait_ge(r_built, (done + 1) * (TOKENS // 2))
                            pe.wait_ge(w_evac, done + 1)
                            for i in range(4):
                                k = 4 * half + i
                                last = nc.tensor.matmul(psum[:, BANKS + half, i * P:(i + 1) * P],
                                                        l_ring[:, k, :], r_ring[:, k, :], start=True, stop=True)
                            last.then_inc(w_product, 1)

            evacuated(pe, ("slots", TB - 1))
            pe.wait_ge(w_evac, 2 + 2 * WSTEPS * TB)
            pe.wait_ge(x_lo_done, TB)

            def hidden(c, k):
                n = c * UNROLL + k
                need(pe, gelu_done, n - UNROLL + 1)
                pe.wait_ge(u_hi_done, n + 1)
                pe.wait_ge(u_lo_done, n + 1)
                for d in range(DC):
                    for w, x, i in ((u_hi, x_hi, 0), (u_hi, x_lo, 1), (u_lo, x_hi, 2)):
                        last = nc.tensor.matmul(psum[:, k, :], w[:, k % 2, d, :], x[:, d, :],
                                                start=(d == 0 and i == 0), stop=(d == DC - 1 and i == 2))
                last.then_inc(h_done, 1)

            def add_up(c, pair, part):
                n = c * UNROLL + 2 * pair
                if part == 0:
                    for s in (v_hi_done, v_lo_done, a_hi_done, a_lo_done):
                        pe.wait_ge(s, n + 2)
                for q in range(4):
                    job = (c * 2 + pair) * GROUP_JOBS + 4 * part + q
                    need(pe, y_evac, job - 3)
                    tb, half = divmod(4 * part + q, 2)
                    passes = [(a, v, 2 * pair + t) for t in range(2)
                              for a, v in ((a_hi, v_hi), (a_hi, v_lo), (a_lo, v_hi))]
                    for i, (a, v, t) in enumerate(passes):
                        last = nc.tensor.matmul(psum[:, 4 + q, :], a[:, t, tb * P:(tb + 1) * P],
                                                v[:, t, half * 512:(half + 1) * 512],
                                                start=(i == 0), stop=(i == len(passes) - 1))
                    last.then_inc(y_done, 1)

            def step(c, first=False):
                hidden(c, 0)
                if not first:
                    add_up(c - 1, 1, 0)
                hidden(c, 1)
                if not first:
                    add_up(c - 1, 1, 1)
                hidden(c, 2)
                add_up(c, 0, 0)
                hidden(c, 3)
                add_up(c, 0, 1)

            step(0, first=True)
            with pe.Fori(1, STEPS) as c:
                step(c)
            add_up(STEPS - 1, 1, 0)
            add_up(STEPS - 1, 1, 1)

        @block.scalar
        def _(act):
            def evac(name, out_ap, in_ap, func=ACT.Copy, **kw):
                produced(act, name)
                nc.scalar.activation(out_ap, in_ap, func, **kw).then_inc(act_evac, 1)

            def ln_std(n):
                act.wait_ge(var_ready, n + 1)
                nc.scalar.activation(std[:, 0:1], mean_var[:, 1:2], ACT.Sqrt, bias=eps[:, :]).then_inc(std_ready, 1)

            act.wait_ge(eps_set, 1)
            for tb in range(TB):
                ln_std(LN_IN + tb)
            for tb in range(TB):
                for half in range(2):
                    evac(("xT", tb, half), xT[:, 4 * half:4 * half + 4, tb * P:(tb + 1) * P],
                         bank(("xT", tb, half)).rearrange("p (j t) -> p j t", j=4))
            for m in range(1, CH_CHUNKS, 2):
                evac(("hT", m), hT[:, m, :], bank(("hT", m)))
            for tb in range(TB):
                evac(("gates", tb), ht[:, tb, DU0:TOKW], bank(("gates", tb)), ACT.Gelu)
            for tb in range(TB):
                ln_std(LN_SGU + tb)
            for n in range(NATT + 1):
                if n < NATT:
                    kind, h, qb, kbs = ATT[n]
                    act.wait_ge(max_ready, n + 1)
                    s = s_sb[:, n % 2, 0:P * len(kbs)]
                    r = row[:, n % 8, :]
                    if kind == "c":
                        nc.scalar.activation(small[:, n % 8:n % 8 + 1], sink_sb[:, h:h + 1], ACT.Exp,
                                             bias=r[:, 1:2]).then_inc(sink_exp_done, 1)
                    nc.scalar.activation(s, s, ACT.Exp, bias=r[:, 1:2], accum_out=r[:, 2:3]).then_inc(exp_done, 1)
                if n >= 1:
                    m = n - 1
                    if m >= 2:
                        produced(act, ("PV", m - 2))
                    w = P * len(ATT[m][3])
                    evac(("PT", m), pT_sb[:, m % 2, 0:w], bank(("PT", m))[:, 0:w])
                if n < NATT and n % 2:
                    name = ("M", n // 2, 1)
                    evac(name, score_w[:, 4:8, (n // 2) * P:(n // 2 + 1) * P],
                         bank(name).rearrange("p (j n) -> p j n", j=4))
            for c in range(2):
                evac(("pool", c), mixT[:, c, :], bank(("pool", c)), scale=pool_scale_sb[:, c:c + 1])
            for c in range(6):
                evac(("mixT", c), mixT[:, 2 + c, :], bank(("mixT", c)))
            for tb in range(TB):
                ln_std(LN_1 + tb)
            act.wait_ge(ln_done, LN_1 + TB)
            act.sem_inc(w_evac, 2)

            def block_of_w(b):
                if b:
                    act.wait_ge(w_stored, 16 * 8 * b)
                with act.Fori(0, WSTEPS) as g:
                    for half in range(2):
                        act.wait_ge(w_product, (g + b * WSTEPS) * 2 + (half + 3))
                        act.sem_inc(w_turn, 1)
                        nc.scalar.activation(
                            wbuf[:, :, bass.ds(g * TOKENS + 4 * half, 4)].rearrange("p i t -> p t i"),
                            psum[:, BANKS + half, :].rearrange("p (t i) -> p t i", t=4), ACT.Copy)\
                            .then_inc(w_evac, 1)

            for tb in range(TB + 1):
                if tb < TB:
                    for half in range(2):
                        chunks = slice(4 * half, 4 * half + 4)
                        src = bank(("x1T", tb, half)).rearrange("p (j t) -> p j t", j=4)
                        produced(act, ("x1T", tb, half))
                        if tb:
                            produced(act, ("sc", tb - 1, 3))
                            act.wait_ge(x_lo_done, tb)
                        nc.scalar.activation(x_hi[:, chunks, tb * P:(tb + 1) * P], src, ACT.Copy)\
                            .then_inc(x_hi_done, 1)
                        evac(("x1T", tb, half), x1T[:, chunks, :], src)
                    act.wait_ge(gate_in, tb + 1)
                    nc.scalar.activation(slots[:, 2, :], slots[:, 2, :], ACT.Exp).then_inc(gate_exp, 1)
                if tb:
                    b = tb - 1
                    if b:
                        act.wait_ge(l_built, P * b + 1)
                        act.wait_ge(r_built, P * b)
                    evac(("slots", b), slotT[:, :, :],
                         bank(("slots", b))[:, 0:3 * P].rearrange("p (i t) -> p i t", i=3))
                    block_of_w(b)
            act.wait_ge(w_stored, 16 * 8 * TB)

            def step(c):
                for k in range(UNROLL):
                    n = c * UNROLL + k
                    turn = c * 2 + k // 2 + 1
                    act.wait_ge(u_raw_loaded[k % 2], turn * 16)
                    need(act, h_done, n - 1)
                    nc.scalar.activation(u_hi[:, k % 2, :, :], u_raw[:, k % 2, :, :], ACT.Copy)\
                        .then_inc(u_hi_done, 1)
                    act.wait_ge(v_raw_loaded[k % 2], turn * 16)
                    need(act, y_done, ((c - 1) * 2 + k // 2 + 1) * GROUP_JOBS)
                    nc.scalar.activation(v_hi[:, k, :], v_raw[:, k % 2, :], ACT.Copy).then_inc(v_hi_done, 1)
                    if isinstance(n, int) and n == 0:
                        continue
                    finish_a(c, k - 1) if k else finish_a(c - 1, UNROLL - 1)

            def finish_a(c, k):
                n = c * UNROLL + k
                act.wait_ge(h_done, n + 1)
                need(act, a_done, n - 1)
                nc.scalar.activation(gelu_h[:, k % 2, :], psum[:, k, :], ACT.Gelu).then_inc(gelu_done, 1)
                act.wait_ge(a_done, n + 1)
                need(act, y_done, ((c - 1) * 2 + k // 2 + 1) * GROUP_JOBS)
                nc.scalar.activation(a_hi[:, k, :], a_full[:, k % 2, :], ACT.Copy).then_inc(a_hi_done, 1)

            step(0)
            with act.Fori(1, STEPS) as c:
                step(c)
            finish_a(STEPS - 1, UNROLL - 1)
            for tb in range(TB):
                ln_std(LN_2 + tb)

        @block.vector
        def _(dve):
            steps = [0]

            def link(ins):
                steps[0] += 1
                ins.then_inc(dve_chain, 1)
                dve.wait_ge(dve_chain, steps[0])

            def evac_done(ins):
                ins.then_inc(dve_evac, 1)

            def layer_norm(n, src, width):
                pieces = max(1, width // 512)
                w = width // pieces
                for i in range(pieces):
                    last = nc.vector.bn_stats(stats[:, i, :], src[:, i * w:(i + 1) * w])
                link(last)
                nc.vector.bn_aggr(mean_var[:, :], stats[:, 0:pieces, :].rearrange("p a b -> p (a b)"))\
                    .then_inc(var_ready, 1)
                dve.wait_ge(std_ready, n + 1)
                link(nc.vector.reciprocal(std[:, 1:2], std[:, 0:1]))
                nc.vector.tensor_scalar(src, src, mean_var[:, 0:1], std[:, 1:2], ALU.subtract, ALU.mult)\
                    .then_inc(scaled_ready, 1)

            for tb in range(TB):
                dve.wait_ge(x_loaded[tb], 16)
                layer_norm(LN_IN + tb, x_sb[:, tb, :], D)
            for i in range(2):
                produced(dve, ("bias", i))
                evac_done(nc.vector.tensor_copy(bias_b[:, 2 * i:2 * i + 2, :],
                                                bank(("bias", i)).rearrange("p (h n) -> p h n", h=2)))
            for m in range(0, CH_CHUNKS, 2):
                produced(dve, ("hT", m))
                evac_done(nc.vector.tensor_copy(hT[:, m, :], bank(("hT", m))))
            for tb in range(TB):
                produced(dve, ("vals", tb))
                evac_done(nc.vector.tensor_copy(ht[:, tb, 0:384], bank(("vals", tb))[:, 0:384]))
            dve.wait_ge(tables_loaded, 16 * N_TABLES)

            for tb in range(TB):
                evacuated(dve, ("gates", tb))
                layer_norm(LN_SGU + tb, ht[:, tb, DV0:DV0 + GROUP], GROUP)

            evacuated(dve, ("hT", A0 + 1))
            for c in range(2):
                a = hT[:, A0 + c, :]
                src, hi = a, 0
                for k in range(4 if c else 2):
                    shift = 1 << k
                    lo = DH if k == (3 if c else 1) else 0
                    dst = s_sb[:, k % 2, :]
                    if lo and k:
                        nc.vector.tensor_copy(dst[0:lo, :], src[0:lo, :])
                    nc.vector.tensor_copy(dst[lo:P, 0:shift], src[lo:P, 0:shift])
                    link(nc.vector.tensor_tensor(dst[lo:P, shift:T], src[lo:P, shift:T], src[lo:P, 0:T - shift],
                                                 ALU.add))
                    src = dst
                link(nc.vector.tensor_tensor(small[:, 0:16], src[:, 0:16], inv_count[:, c, :], ALU.mult))
                link(nc.vector.tensor_tensor(small[:, 0:16], small[:, 0:16], a[:, 0:16], ALU.subtract))
                for g in range(2):
                    lo = DH * g
                    w = POOL_WINDOWS[2 * c + g]
                    last = nc.vector.scalar_tensor_tensor(out=a[lo:lo + DH, 16:T], in0=src[lo:lo + DH, 16:T],
                                                          scalar=1.0 / w, in1=a[lo:lo + DH, 16:T],
                                                          op0=ALU.mult, op1=ALU.subtract)
                link(last)
                link(nc.vector.tensor_copy(a[:, 0:16], small[:, 0:16]))
                nc.vector.tensor_copy(small[:, 0:1], small[:, 0:1]).then_inc(pooled, 1)

            dve.wait_ge(masks_set, 2)
            cs = 0
            for n in range(NATT + 2):
                if n < NATT:
                    kind, h, qb, kbs = ATT[n]
                    ps = bank(("S", n))
                    produced(dve, ("S", n))
                    if n >= 2:
                        produced(dve, ("PT", n - 2))
                    s = s_sb[:, n % 2, :]
                    r = row[:, n % 8, :]
                    near = min(2, len(kbs))
                    far = P * (len(kbs) - near)
                    bias = bias_b if kind == "b" else alibi
                    if far:
                        nc.vector.tensor_scalar(s[:, 0:far], ps[:, 0:far], SCALE, bias_b[:, h, 0:1],
                                                ALU.mult, ALU.add)
                    last = nc.vector.scalar_tensor_tensor(
                        out=s[:, far:far + P * near], in0=ps[:, far:far + P * near], scalar=SCALE,
                        in1=bias[:, h, 256 - P * near:256], op0=ALU.mult, op1=ALU.add)
                    evac_done(last)
                    dve.wait_ge(dve_evac, evacuations(JOB_AT[("S", n)] + 1)["dve"])
                    link(nc.vector.reduce_max(r[:, 0:1], s[:, 0:far + P * near], AX.X))
                    if kind == "c":
                        link(nc.vector.tensor_tensor(r[:, 0:1], r[:, 0:1], sink_sb[:, h:h + 1], ALU.max))
                    nc.vector.tensor_scalar(r[:, 1:2], r[:, 0:1], -1.0, None, ALU.mult).then_inc(max_ready, 1)
                if n >= 2:
                    m = n - 2
                    kind, h, qb, kbs = ATT[m]
                    r = row[:, m % 8, :]
                    dve.wait_ge(exp_done, m + 1)
                    if kind == "c":
                        cs += 1
                        dve.wait_ge(sink_exp_done, cs)
                        link(nc.vector.tensor_tensor(r[:, 2:3], r[:, 2:3], small[:, m % 8:m % 8 + 1], ALU.add))
                    link(nc.vector.reciprocal(r[:, 3:4], r[:, 2:3]))
                    produced(dve, ("PV", m))
                    col = (0 if kind == "b" else GROUP) + DH * h
                    evac_done(nc.vector.tensor_scalar(mix_tok[:, qb, col:col + DH], bank(("PV", m))[:, 0:DH],
                                                      r[:, 3:4], None, ALU.mult))
                if n < NATT and n % 2 == 0:
                    name = ("M", n // 2, 0)
                    produced(dve, name)
                    evac_done(nc.vector.tensor_copy(score_w[:, 0:4, (n // 2) * P:(n // 2 + 1) * P],
                                                    bank(name).rearrange("p (j n) -> p j n", j=4)))
            for tb in range(TB):
                produced(dve, ("sgu", tb))
                for g in range(HEADS):
                    last = nc.vector.scalar_tensor_tensor(
                        out=ht[:, tb, DU0 + g * DH:DU0 + (g + 1) * DH],
                        in0=bank(("sgu", tb))[:, g * DH:(g + 1) * DH], scalar=sgu_b_sb[:, g:g + 1],
                        in1=ht[:, tb, DU0 + g * DH:DU0 + (g + 1) * DH], op0=ALU.add, op1=ALU.mult)
                evac_done(last)
            for tb in range(TB):
                for half in range(2):
                    produced(dve, ("out", tb, half))
                    cols = slice(half * 512, (half + 1) * 512)
                    evac_done(nc.vector.scalar_tensor_tensor(
                        out=x_sb[:, tb, cols], in0=x_sb[:, tb, cols], scalar=ALPHA,
                        in1=bank(("out", tb, half)), op0=ALU.mult, op1=ALU.add))
                evacuated(dve, ("out", tb, 1))
                layer_norm(LN_1 + tb, x_sb[:, tb, :], D)
            dve.wait_ge(ln_done, LN_1 + TB)

            def top16(values, indices, scores, scratch, evacuates=False):
                link(nc.vector.max(values[:, 0:8], scores))
                nc.vector.max_index(indices[:, 0:8], values[:, 0:8], scores)
                last = nc.vector.match_replace(scratch, values[:, 0:8], scores, LOWEST)
                if evacuates:
                    evac_done(last)
                    dve.wait_ge(dve_evac, evacuates)
                else:
                    link(last)
                link(nc.vector.max(values[:, 8:16], scratch))
                link(nc.vector.max_index(indices[:, 8:16], values[:, 8:16], scratch))

            def route_block(tb):
                for g in range(4):
                    name = ("sc", tb, g)
                    produced(dve, name)
                    for j in range(4):
                        m = 4 * g + j
                        count = evacuations(JOB_AT[name] + 1)["dve"] if j == 3 else False
                        top16(topv[:, 16 * m:16 * m + 16], topi[:, 16 * m:16 * m + 16],
                              bank(name)[:, j * P:(j + 1) * P], work[:, 0:P], count)
                tv = topv.rearrange("p (h z k) -> p h z k", h=PH, z=2)
                tf = topi_f.rearrange("p (h z k) -> p h z k", h=PH, z=2)
                c4 = cand.rearrange("p (h a b) -> p h a b", h=PH, a=TOPK)
                link(nc.vector.tensor_copy(topi_f, topi))
                shape = [P, PH, TOPK, TOPK]
                link(nc.vector.tensor_tensor(c4, tv[:, :, 0, :].unsqueeze(3).to_broadcast(shape),
                                             tv[:, :, 1, :].unsqueeze(2).to_broadcast(shape), ALU.add))
                for h in range(PH):
                    top16(best[:, 16 * h:16 * h + 16], pos[:, 16 * h:16 * h + 16],
                          cand[:, 256 * h:256 * h + 256], work)
                for z, where in enumerate((pos_a, pos_b)):
                    op, n = ((ALU.logical_shift_right, 4), (ALU.bitwise_and, 15))[z]
                    link(nc.vector.tensor_scalar(where, pos, n, None, op))
                if tb:
                    produced(dve, ("slots", tb - 1))
                hot4 = hot.rearrange("p (h k a) -> p h k a", h=PH, k=TOPK)
                hot3 = hot.rearrange("p (s a) -> p s a", a=TOPK)
                for z, where in enumerate((pos_a, pos_b)):
                    key = slots[:, z, :]
                    link(nc.vector.tensor_copy(key, where))
                    link(nc.vector.tensor_tensor(hot3, key.unsqueeze(2).to_broadcast([P, NSEL, TOPK]),
                                                 iota[:, 0:TOPK].unsqueeze(1).to_broadcast([P, NSEL, TOPK]),
                                                 ALU.is_equal))
                    link(nc.vector.tensor_tensor(hot4, hot4, tf[:, :, z, :].unsqueeze(2).to_broadcast(shape),
                                                 ALU.mult))
                    link(nc.vector.tensor_reduce(key, hot3, AX.X, ALU.add))
                g3 = slots[:, 2, :].rearrange("p (h k) -> p h k", h=PH)
                b3 = best.rearrange("p (h k) -> p h k", h=PH)
                nc.vector.tensor_tensor(g3, b3, b3[:, :, 0:1].to_broadcast([P, PH, TOPK]), ALU.subtract)\
                    .then_inc(gate_in, 1)
                dve.wait_ge(gate_exp, tb + 1)
                link(nc.vector.tensor_reduce(small[:, 0:PH], g3, AX.X, ALU.add))
                link(nc.vector.reciprocal(small[:, 8:8 + PH], small[:, 0:PH]))
                nc.vector.tensor_tensor(g3, g3, small[:, 8:8 + PH].unsqueeze(2).to_broadcast([P, PH, TOPK]),
                                        ALU.mult).then_inc(slots_ready, 1)

            def one_hot_rows(b):
                evacuated(dve, ("slots", b))
                with dve.Fori(0, WSTEPS) as g:
                    for k in range(TOKENS):
                        if k % 4 == 0:
                            dve.wait_ge(w_product, (g + b * WSTEPS) * 2 + (k // 4 + 1))
                        nc.vector.tensor_scalar(r_ring[:, k, :], iota[:, :],
                                                slotT[:, 0, bass.ds(g * TOKENS + k, 1)], None,
                                                ALU.is_equal).then_inc(r_built, 1)

            for tb in range(TB + 1):
                if tb < TB:
                    route_block(tb)
                if tb:
                    one_hot_rows(tb - 1)

            for tb in range(TB):
                produced(dve, ("x1T", tb, 1))
                last = nc.vector.tensor_scalar(x_sb[:, tb, :], x_sb[:, tb, :], ALPHA, None, ALU.mult)
            link(last)

            def low_u(c, k):
                n = c * UNROLL + k
                dve.wait_ge(u_hi_done, n + 1)
                nc.vector.tensor_tensor(u_lo[:, k % 2, :, :], u_raw[:, k % 2, :, :],
                                        u_hi[:, k % 2, :, :].bitcast(F32), ALU.subtract).then_inc(u_lo_done, 1)

            def make_a(c, k):
                n = c * UNROLL + k
                dve.wait_ge(w_tile_loaded[k], (c + 1) * 16)
                dve.wait_ge(gelu_done, n + 1)
                need(dve, a_hi_done, n - 1)
                need(dve, a_lo_done, n - 1)
                nc.vector.tensor_tensor(a_full[:, k % 2, :], w_tile[:, k, :], gelu_h[:, k % 2, :], ALU.mult)\
                    .then_inc(a_done, 1)
                dve.wait_ge(a_hi_done, n + 1)
                nc.vector.tensor_tensor(a_lo[:, k, :], a_full[:, k % 2, :], a_hi[:, k, :].bitcast(F32),
                                        ALU.subtract).then_inc(a_lo_done, 1)

            def add_y(c, pair, part):
                for q in range(4):
                    job = (c * 2 + pair) * GROUP_JOBS + 4 * part + q
                    tb, half = divmod(4 * part + q, 2)
                    y = x_sb[:, tb, half * 512:(half + 1) * 512]
                    need(dve, y_evac, job - GROUP_JOBS + 1)
                    dve.wait_ge(y_done, job + 1)
                    nc.vector.tensor_tensor(y, y, psum[:, 4 + q, :], ALU.add).then_inc(y_evac, 1)

            def step(c, first=False):
                low_u(c, 0)
                if not first:
                    make_a(c - 1, 3)
                low_u(c, 1)
                if not first:
                    add_y(c - 1, 1, 0)
                make_a(c, 0)
                low_u(c, 2)
                if not first:
                    add_y(c - 1, 1, 1)
                make_a(c, 1)
                low_u(c, 3)
                add_y(c, 0, 0)
                make_a(c, 2)
                add_y(c, 0, 1)

            step(0, first=True)
            with dve.Fori(1, STEPS) as c:
                step(c)
            make_a(STEPS - 1, 3)
            add_y(STEPS - 1, 1, 0)
            add_y(STEPS - 1, 1, 1)
            dve.wait_ge(y_evac, 2 * STEPS * GROUP_JOBS)
            for tb in range(TB):
                layer_norm(LN_2 + tb, x_sb[:, tb, :], D)

        @block.gpsimd
        def _(pool):
            steps = [0]

            def link(ins):
                steps[0] += 1
                ins.then_inc(pool_chain, 1)
                pool.wait_ge(pool_chain, steps[0])

            def gain_bias(n, src, g, b):
                pool.wait_ge(scaled_ready, n + 1)
                link(nc.gpsimd.tensor_tensor(src, src, g, ALU.mult))
                nc.gpsimd.tensor_tensor(src, src, b, ALU.add).then_inc(ln_done, 1)

            nc.gpsimd.memset(eps[:, :], EPS).then_inc(eps_set, 1)
            pool.wait_ge(ln_in_loaded, 32)
            for tb in range(TB):
                gain_bias(LN_IN + tb, x_sb[:, tb, :], lnv[0], lnv[1])
            pool.wait_ge(sgu_w_loaded, 48)
            nc.gpsimd.affine_select(out=sgu_w_sb, in_=sgu_w_sb, compare_op=ALU.is_ge, fill=0.0,
                                    base=0, pattern=[[0, HEADS], [1, P]], channel_multiplier=-1)\
                .then_inc(masks_set, 1)
            evacuated(pool, ("bias", 1))
            nc.gpsimd.memset(bias_b[0:CHUNK, :, 256 - CHUNK:256], NEG).then_inc(masks_set, 1)
            pool.wait_ge(tables_loaded, 16 * N_TABLES)
            for tb in range(TB):
                gain_bias(LN_SGU + tb, ht[:, tb, DV0:DV0 + GROUP], lnv_sgu[:, 0, :], lnv_sgu[:, 1, :])
            for tb in range(TB):
                gain_bias(LN_1 + tb, x_sb[:, tb, :], lnv[2], lnv[3])

            def low_x(tb):
                for half in range(2):
                    chunks = slice(4 * half, 4 * half + 4)
                    evacuated(pool, ("x1T", tb, half))
                    last = nc.gpsimd.tensor_tensor(x_lo[:, chunks, tb * P:(tb + 1) * P], x1T[:, chunks, :],
                                                   x_hi[:, chunks, tb * P:(tb + 1) * P].bitcast(F32),
                                                   ALU.subtract)
                last.then_inc(x_lo_done, 1)

            def gate_rows(b):
                evacuated(pool, ("slots", b))
                with pool.Fori(0, WSTEPS) as g:
                    pool.wait_ge(l_built, (g + b * WSTEPS) * TOKENS + 1)
                    pool.sem_inc(pool_turn, 1)
                    nc.gpsimd.tensor_copy(staged[:, :, :],
                                          slotT[:, 1:3, bass.ds(g * TOKENS, TOKENS)]).then_inc(slots_staged, 1)
                    pool.wait_ge(slots_staged, g + (b * WSTEPS + 1))
                    for k in range(TOKENS):
                        if k % 4 == 0:
                            pool.wait_ge(w_product, (g + b * WSTEPS) * 2 + (k // 4 + 1))
                            pool.sem_inc(pool_turn, 1)
                        nc.gpsimd.tensor_scalar(l_ring[:, k, :], iota[:, :], staged[:, 0, k:k + 1],
                                                staged[:, 1, k:k + 1], ALU.is_equal, ALU.mult).then_inc(l_built, 1)

            pool.sem_inc(l_built, 1)
            for tb in range(TB + 1):
                if tb < TB:
                    low_x(tb)
                if tb:
                    gate_rows(tb - 1)

            def low_v(c):
                for k in range(UNROLL):
                    n = c * UNROLL + k
                    pool.wait_ge(v_hi_done, n + 1)
                    nc.gpsimd.tensor_tensor(v_lo[:, k, :], v_raw[:, k % 2, :], v_hi[:, k, :].bitcast(F32),
                                            ALU.subtract).then_inc(v_lo_done, 1)

            with pool.Fori(0, STEPS) as c:
                low_v(c)
            pool.wait_ge(ln2_loaded, 32)
            for tb in range(TB):
                gain_bias(LN_2 + tb, x_sb[:, tb, :], ln2_vectors[:, 0, :], ln2_vectors[:, 1, :])


def shape_constants():
    i = np.arange(P)[:, None]
    u = np.arange(2 * P)[None, :]
    dist = np.abs(P + i - u).astype(np.float32)
    key_chunk = u // CHUNK
    own = 2 + i // CHUNK
    seen = (key_chunk == own) | (key_chunk == own - 1)
    slopes = 2.0 ** (-8.0 * (np.arange(HEADS, dtype=np.float32) + 1.0) / HEADS)
    alibi = np.where(seen[:, None, :], -slopes[None, :, None] * dist[:, None, :], NEG).astype(np.float32)
    inv = np.zeros((P, 2, 16), np.float32)
    for g, w in enumerate(POOL_WINDOWS):
        inv[DH * (g % 2):DH * (g % 2) + DH, g // 2, :] = 1.0 / np.minimum(np.arange(16) + 1, w)
    iota = np.tile(np.arange(P, dtype=np.float32), (P, 1))
    return np.eye(P, dtype=np.float32), alibi, inv, iota


def kernel(**inputs):
    import concourse.bacc as bacc
    from concourse.bass_utils import run_bass_kernel_spmd

    a = {k: np.asarray(v) for k, v in inputs.items()}
    w_in = a["w_in"][0]
    cq = [1024 + DH * h + np.arange(DH) for h in C_HEAD_AT]
    order = np.concatenate([np.arange(0, 768), *cq, np.arange(1280, 1408),
                            np.arange(768, 1024), np.arange(1408, 1536), np.arange(1536, 2048)])
    rel_at = np.clip(256 - np.arange(512), -REL_CLIP, REL_CLIP) + REL_CLIP
    ident, alibi, inv, iota = shape_constants()
    arrays = {
        "x": a["x"].reshape(T, D),
        "w_in": w_in[:, order],
        "w_out": a["w_out"][0],
        "pool_lin": a["pool_lin"][0].reshape(2, 2, DH, DH).transpose(1, 2, 0, 3).reshape(P, 2, DH),
        "pool_scale": a["pool_scale"][0].reshape(2, P).T,
        "rel_ext": a["rel_bias"][0][:, rel_at],
        "sinks": a["sinks"][0],
        "sgu_ln_g": a["sgu_ln_g"][0],
        "sgu_ln_b": a["sgu_ln_b"][0],
        "sgu_wT": a["sgu_w"][0].transpose(2, 0, 1),
        "sgu_bT": a["sgu_b"][0].T,
        "ln_in_g": a["ln_in_g"], "ln_in_b": a["ln_in_b"],
        "ln1_g": a["ln1_g"][0], "ln1_b": a["ln1_b"][0],
        "ln2_g": a["ln2_g"][0], "ln2_b": a["ln2_b"][0],
        "wq_keys": np.concatenate([a["peer_wq"][0].reshape(D, NHZ, P).transpose(1, 2, 0),
                                   a["peer_keys"][0].reshape(NHZ, NKEYS, P).transpose(0, 2, 1)], axis=2),
        "expert_uT": a["expert_u"][0].reshape(TILES, P, DC, P).transpose(0, 3, 2, 1).reshape(TILES * P, D),
        "expert_v": a["expert_v"][0],
        "identity_c": ident, "flip_c": ident[::-1], "alibi_c": alibi, "inv_count_c": inv, "iota_c": iota,
    }
    nc = bacc.Bacc("TRN2", target_bir_lowering=False, num_devices=1)
    arrays = {f"in_{k}": np.ascontiguousarray(v) for k, v in arrays.items()}
    args = [nc.dram_tensor(k, v.shape, mybir.dt.from_np(v.dtype), kind="ExternalInput").ap()
            for k, v in arrays.items()]
    out = nc.dram_tensor("out", (T, D), F32, kind="ExternalOutput").ap()
    w_dram = nc.dram_tensor("w_scratch", (TILES, P, T), F32).ap()
    hybrid_layer(nc, *args, w_dram, out)
    r = run_bass_kernel_spmd(nc, [arrays], core_ids=[0])
    return r.results[0]["out"].reshape(1, T, D)
```

```python
from contextlib import ExitStack

import numpy as np
import concourse.bass as bass
from concourse import mybir

F32 = mybir.dt.float32
F32R = mybir.dt.float32r
U32 = mybir.dt.uint32
ALU = mybir.AluOpType
ACT = mybir.ActivationFunctionType
AX = mybir.AxisListType

P = 128
T = 512
D = 1024
TB = T // P
DC = D // P
GROUP = 256
DH = 64
HEADS = 4
CHUNK = 64
POOL_WINDOWS = (2, 4, 8, 16)
REL_CLIP = 128
ALPHA = 2.0 ** 0.25
EPS = 1e-5
NEG = -1e30
SCALE = DH ** -0.5
LOWEST = -3.0e38
PH = 8
TOPK = 16
NKEYS = 128
NHZ = 2 * PH
NSEL = PH * TOPK
TOKENS = 16
QUARTERS = TOKENS // 4
WSTEPS = P // TOKENS
TILES = NKEYS
UNROLL = 4
STEPS = TILES // UNROLL
GROUP_JOBS = 2 * TB
AHEAD = TILES // 2
BEFORE_W = (8, 8, 8, 8)
AHEAD_AT = tuple(sum(BEFORE_W[:b + 1]) + WSTEPS * b for b in range(TB))
SLOTS_BANK = 4
PIECES = 8

CH_CHUNKS = 9
A0, BQ0, BK0, CQ0, CK0 = 0, 2, 4, 6, 8
BV0, CV0, DU0, DV0 = 0, 256, 384, 640
TOKW = 896
C_HEAD_AT = (0, 2, 1, 3)
BANKS = 6


def attention_tiles():
    tiles = []
    for h in range(HEADS):
        for qb in range(TB):
            tiles.append(("b", h, qb, list(range(qb + 1))))
            tiles.append(("c", h, qb, list(range(max(0, qb - 1), qb + 1))))
    return tiles


ATT = attention_tiles()
NATT = len(ATT)


OUT_ORDER = [("out", 0), ("out", 1), ("x1T", 0), ("out", 2), ("x1T", 1), ("out", 3), ("x1T", 2), ("x1T", 3)]


def psum_jobs():
    jobs = []
    for tb in range(TB):
        jobs += [(("xT", tb, half), "dve") for half in range(2)]
    for c in range(CH_CHUNKS):
        jobs.append((("hT", c), "act" if c % 2 else "dve"))
        if c == 3:
            jobs += [(("bias", i), "dve") for i in range(2)]
    jobs += [(("vals", tb), "dve") for tb in range(TB)]
    jobs += [(("gates", tb), "act") for tb in range(TB)]
    jobs.insert(len(jobs) - 1, (("S", 0), "dve"))
    for n in range(NATT + 3):
        if 1 <= n < NATT:
            jobs.append((("S", n), "dve"))
        if 2 <= n < NATT + 2:
            jobs.append((("PT", n - 2), "act"))
        if n >= 3:
            jobs.append((("PV", n - 3), "dve"))
    jobs += [(("pool", c), "act") for c in range(2)]
    jobs += [(("sgu", tb), "dve") for tb in range(TB)]
    jobs += [(("mixT", c), "act") for c in range(6)]
    for what, tb in OUT_ORDER:
        jobs += [((what, tb, half), "dve") for half in range(2)]
    return jobs


JOBS = psum_jobs()
assert sum(BEFORE_W) + WSTEPS * TB == AHEAD
assert UNROLL == 4 and min(BEFORE_W[1:]) >= PIECES and all(n % 2 == 0 for n in BEFORE_W)
JOB_AT = {name: n for n, (name, _) in enumerate(JOBS)}


def need(eng, semaphore, value):
    if not isinstance(value, int) or value > 0:
        eng.wait_ge(semaphore, value)


def evacuations(upto):
    return {e: sum(1 for _, x in JOBS[:upto] if x == e) for e in ("act", "dve")}


def hybrid_layer(nc, x, w_in, w_out, pool_lin, pool_scale, rel_ext, sinks, sgu_ln_g, sgu_ln_b, sgu_wT,
                 sgu_bT, ln_in_g, ln_in_b, ln1_g, ln1_b, ln2_g, ln2_b, wqT, keysT, expert_uT, expert_v,
                 identity_c, flip_c, alibi_c, inv_count_c, iota_c, w_dram, g_dram, out):
    with ExitStack() as ctx:
        def sb(name, shape, dt=F32):
            return ctx.enter_context(nc.sbuf_tensor(name, shape, dt))

        def sem(name):
            return ctx.enter_context(nc.semaphore(name))

        x_sb = sb("x_sb", [P, TB, D])
        ident = sb("ident", [P, P])
        iota = sb("iota", [P, P])
        stats = sb("stats", [P, 2, 6])
        mean_var = sb("mean_var", [P, 2])
        std = sb("std", [P, 2])
        eps = sb("eps", [P, 1])
        row = sb("row", [P, 8, 4])
        small = sb("small", [P, 16])
        pool_scale_sb = sb("pool_scale_sb", [P, 2])
        sink_sb = sb("sink_sb", [P, HEADS])
        sgu_b_sb = sb("sgu_b_sb", [P, HEADS])

        with ExitStack() as low:
            with ExitStack() as project:
                w_in_hi, w_in_lo = (project.enter_context(nc.sbuf_tensor(name, [P, 2, DC, 512], F32R))
                                    for name in ("w_in_hi", "w_in_lo"))
            low.enter_context(nc.sbuf_tensor("experts_place", [P, DC * 2048], F32))
            with ExitStack() as front:
                def fb(name, shape, dt=F32):
                    return front.enter_context(nc.sbuf_tensor(name, shape, dt))

                hT = fb("hT", [P, CH_CHUNKS, T])
                ht = fb("ht", [P, TB, TOKW])
                with ExitStack() as project:
                    x_in_hi, x_in_lo = (project.enter_context(nc.sbuf_tensor(name, [P, DC, T], F32R))
                                        for name in ("x_in_hi", "x_in_lo"))
                mix_tok = fb("mix_tok", [P, TB, 2 * GROUP])
                mixT = fb("mixT", [P, DC, T])
                fb("rest_of_x_in_lo", [P, 1024])
                s_more = fb("s_more", [P, 2, T])
                w_out_sb = fb("w_out_sb", [P, DC, D])
                ln_vectors = fb("ln_vectors", [P, 4, D])
                lnv = [ln_vectors[:, i, :] for i in range(4)]
                bias_b = fb("bias_b", [P, HEADS, 256])
                s_sb = fb("s_sb", [P, 2, T])
                pT_sb = fb("pT_sb", [P, 2, T])
                pool_lin_sb = fb("pool_lin_sb", [P, 2, DH])
                inv_count = fb("inv_count", [P, 2, 16])
            w_in_raw = w_out_sb[:, :, :].rearrange("p c n -> p (c n)").rearrange("p (s c n) -> p s c n", s=2, c=DC)
            flip = pT_sb[:, 0, 0:P]
            alibi = lnv[1].rearrange("p (h n) -> p h n", h=HEADS)
            sgu_w_sb = lnv[0][:, 0:HEADS * P].rearrange("p (g t) -> p g t", g=HEADS)
            lnv_sgu = lnv[0][:, 512:1024].rearrange("p (i n) -> p i n", i=2)

            with ExitStack() as route:
                def rb(name, shape, dt=F32):
                    return route.enter_context(nc.sbuf_tensor(name, shape, dt))

                rb("x_halves", [P, 2, DC, T])
                wbuf = rb("wbuf", [P, TILES, P])
                cand = rb("cand", [P, PH * TOPK * TOPK])
                topi_ft = rb("topi_ft", [P, NHZ * TOPK])
                work_t = rb("work_t", [P, 4 * NKEYS])
                best_t = rb("best_t", [P, NSEL])
                pos_t = rb("pos_t", [P, 3, NSEL], U32)
                slots = rb("slots", [P, 3, NSEL])
                slotT = rb("slotT", [P, 3, P])
                l_ring = rb("l_ring", [P, TOKENS, P])
            topi_f, work = topi_ft[:, :], work_t[:, :]
            r_ring = cand[:, :].rearrange("p (t i) -> p t i", t=TOKENS)
            hot = cand[:, 0:PH * TOPK * TOPK]
            best = best_t[:, :]
            pos, pos_a, pos_b = (pos_t[:, i, :] for i in range(3))

            with ExitStack() as dense:
                def db(name, shape, dt=F32):
                    return dense.enter_context(nc.sbuf_tensor(name, shape, dt))

                x_hi = db("x_hi", [P, DC, T], F32R)
                x_lo = db("x_lo", [P, DC, T], F32R)
                db("wbuf_place", [P, TILES, P])
                a_hi = db("a_hi", [P, UNROLL, T], F32R)
                a_lo = db("a_lo", [P, UNROLL, T], F32R)
                w_tile = db("w_tile", [P, UNROLL, T - P])
                a_full = db("a_full", [P, 2, T])
                g_tile = db("g_tile", [P, 2, T])
            with ExitStack() as last:
                ln2_vectors = last.enter_context(nc.sbuf_tensor("ln2_vectors", [P, 2, D], F32))
        with ExitStack() as low:
            def eb(name, shape, dt=F32):
                return low.enter_context(nc.sbuf_tensor(name, shape, dt))

            u_raw = eb("u_raw", [P, 2, DC, P])
            u_hi = eb("u_hi", [P, 2, DC, P], F32R)
            u_lo = eb("u_lo", [P, 2, DC, P], F32R)
            with ExitStack() as ahead:
                topv_all = ahead.enter_context(nc.sbuf_tensor("topv_all", [P, TB, NHZ * TOPK], F32))
                topi_all = ahead.enter_context(nc.sbuf_tensor("topi_all", [P, TB, NHZ * TOPK], U32))
                keys_sb = ahead.enter_context(nc.sbuf_tensor("keys_sb", [P, NHZ, NKEYS], F32))
                q_sb = ahead.enter_context(nc.sbuf_tensor("q_sb", [P, 2, T], F32))
                ahead.enter_context(nc.sbuf_tensor("v_hi_rest", [P, 3072], F32))
                g_stage = ahead.enter_context(nc.sbuf_tensor("g_stage", [P, 2, T], F32))
            v_raw = eb("v_raw", [P, 2, D])
            v_hi = eb("v_hi", [P, UNROLL, D], F32R)
            v_lo = eb("v_lo", [P, UNROLL, D], F32R)

        psum = ctx.enter_context(nc.psum_tensor("psum", [P, 8, 512], F32))

        x_loaded = [sem(f"x_loaded{t}") for t in range(TB)]
        alibi_loaded = sem("alibi_loaded")
        x_in_hi_done = sem("x_in_hi_done")
        w_in_hi_done = sem("w_in_hi_done")
        w_in_lo_done = sem("w_in_lo_done")
        w_in_loaded = [sem(f"w_in_loaded{c}") for c in range(4)]
        ln_in_loaded = sem("ln_in_loaded")
        ident_loaded = sem("ident_loaded")
        tables_loaded = sem("tables_loaded")
        bias_loaded = sem("bias_loaded")
        sgu_w_loaded = sem("sgu_w_loaded")
        w_out_loaded = sem("w_out_loaded")
        keys_loaded = sem("keys_loaded")
        sc_done = sem("sc_done")
        sc_evac = sem("sc_evac")
        ln2_loaded = sem("ln2_loaded")
        pe_job = sem("pe_job")
        act_evac = sem("act_evac")
        dve_evac = sem("dve_evac")
        dve_chain = sem("dve_chain")
        eps_set = sem("eps_set")
        masks_set = sem("masks_set")
        var_ready = sem("var_ready")
        std_ready = sem("std_ready")
        ln_done = sem("ln_done")
        max_ready = sem("max_ready")
        exp_done = sem("exp_done")
        sink_exp_done = sem("sink_exp_done")
        pooled = sem("pooled")
        gate_in = sem("gate_in")
        gate_exp = sem("gate_exp")
        slots_ready = sem("slots_ready")
        x_hi_done = sem("x_hi_done")
        l_built = sem("l_built")
        r_built = sem("r_built")
        w_product = sem("w_product")
        w_evac = sem("w_evac")
        w_turn = sem("w_turn")
        slots_transposed = sem("slots_transposed")
        slots_evac = sem("slots_evac")
        g_stored = [sem(f"g_stored{s}") for s in range(2)]
        g_tile_loaded = [sem(f"g_tile_loaded{s}") for s in range(2)]
        w_stored = sem("w_stored")
        u_raw_loaded = [sem(f"u_raw_loaded{s}") for s in range(2)]
        v_raw_loaded = [sem(f"v_raw_loaded{s}") for s in range(2)]
        w_tile_loaded = [sem(f"w_tile_loaded{s}") for s in range(UNROLL)]
        u_hi_done = sem("u_hi_done")
        u_lo_done = sem("u_lo_done")
        v_hi_done = sem("v_hi_done")
        v_lo_done = sem("v_lo_done")
        h_done = sem("h_done")
        h_taken = sem("h_taken")
        a_done = sem("a_done")
        a_hi_done = sem("a_hi_done")
        a_lo_done = sem("a_lo_done")
        y_done = sem("y_done")
        y_evac = sem("y_evac")
        stored = sem("stored")

        def s_tile(n):
            return (s_more if n & 2 else s_sb)[:, n % 2, :]

        evac_sem = {"act": act_evac, "dve": dve_evac}

        def bank(name):
            return psum[:, JOB_AT[name] % BANKS, :]

        def produced(eng, name):
            eng.wait_ge(pe_job, JOB_AT[name] + 1)

        def evacuated(eng, name):
            n = JOB_AT[name]
            e = JOBS[n][1]
            eng.wait_ge(evac_sem[e], evacuations(n + 1)[e])

        def tile_of(c, k):
            return c * 2 + (AHEAD + k if k < 2 else k - 2)

        LN_IN, LN_SGU, LN_1, LN_2 = 0, 4, 8, 12
        N_TABLES = 8

        block = ctx.enter_context(nc.Block())

        @block.sync
        def _(sp):
            def bcast(dst, src, done):
                n = src.shape[0]
                sp.dma_start(dst, src.rearrange("(a n) -> a n", a=1).to_broadcast([P, n])).then_inc(done, 16)

            sp.dma_start(ident[:, :], identity_c).then_inc(ident_loaded, 16)
            for tb in range(TB):
                sp.dma_start(x_sb[:, tb, :], x[tb * P:(tb + 1) * P, :]).then_inc(x_loaded[tb], 16)
                if tb == 0:
                    bcast(lnv[0], ln_in_g, ln_in_loaded)
                    bcast(lnv[1], ln_in_b, ln_in_loaded)
            for i in range(4):
                cols = slice(i * 512, (i + 1) * 512)
                need(sp, w_in_lo_done, 4 * (i - 1))
                sp.dma_start(w_in_raw[:, i % 2, :, :], w_in[:, cols].rearrange("(c p) n -> p c n", p=P))\
                    .then_inc(w_in_loaded[i], 16)
                if i == 1:
                    sp.dma_start(flip, flip_c).then_inc(bias_loaded, 16)
                    for h in range(HEADS):
                        src = bass.AP(tensor=rel_ext.tensor, offset=h * 512 + 1, ap=[[1, P], [1, 256]])
                        sp.dma_start(s_sb[:, h // 2, (h % 2) * 256:(h % 2) * 256 + 256], src)\
                            .then_inc(bias_loaded, 16)
            sp.dma_start(pool_lin_sb[:, :, :], pool_lin).then_inc(tables_loaded, 16)
            sp.dma_start(pool_scale_sb[:, :], pool_scale).then_inc(tables_loaded, 16)
            sp.dma_start(inv_count[:, :, :], inv_count_c).then_inc(tables_loaded, 16)
            sp.dma_start(iota[:, :], iota_c).then_inc(tables_loaded, 16)
            bcast(sink_sb[:, :], sinks, tables_loaded)
            sp.dma_start(sgu_b_sb[:, :], sgu_bT).then_inc(tables_loaded, 16)
            bcast(lnv[2], ln1_g, tables_loaded)
            bcast(lnv[3], ln1_b, tables_loaded)
            sp.wait_ge(w_in_lo_done, DC * 2)
            sp.dma_start(w_out_sb[:, :, :], w_out.rearrange("(c p) n -> p c n", p=P)).then_inc(w_out_loaded, 16)
            sp.wait_ge(ln_done, LN_IN + TB)
            sp.dma_start(alibi, alibi_c).then_inc(alibi_loaded, 16)
            sp.dma_start(sgu_w_sb, sgu_wT).then_inc(sgu_w_loaded, 16)
            bcast(lnv_sgu[:, 0, :], sgu_ln_g, sgu_w_loaded)
            bcast(lnv_sgu[:, 1, :], sgu_ln_b, sgu_w_loaded)
            w_rows = w_dram.rearrange("i j t -> (i j) t")

            g_rows = g_dram.rearrange("i j t -> (i j) t")

            def load_wq(m):
                need(sp, u_lo_done, m - 1)
                sp.dma_start(u_raw[:, m % 2, :, :].rearrange("p c e -> p (c e)"),
                             wqT[m * P:(m + 1) * P, :]).then_inc(u_raw_loaded[m % 2], 16)

            def load_u(h, s):
                n = h * 2 + s
                sp.wait_ge(u_lo_done, n + (NHZ - 1))
                sp.dma_start(u_raw[:, s, :, :].rearrange("p c e -> p (c e)"),
                             expert_uT[bass.ds(n * P, P), :]).then_inc(u_raw_loaded[s], 16)

            def store_g(h, s):
                n = h * 2 + s
                sp.wait_ge(h_taken, n + (NHZ + 1))
                sp.dma_start(g_rows[bass.ds(n * P, P), :], g_stage[:, s, :]).then_inc(g_stored[s], 16)

            def load_v(c, k):
                need(sp, v_lo_done, c * UNROLL + k - 1)
                sp.dma_start(v_raw[:, k % 2, :], expert_v[bass.ds(tile_of(c, k) * P, P), :])\
                    .then_inc(v_raw_loaded[k % 2], 16)

            def load_w(c, k):
                need(sp, a_done, (c - 1) * UNROLL + k + 1)
                sp.dma_start(w_tile[:, k, :], w_rows[bass.ds(tile_of(c, k) * P, P), :])\
                    .then_inc(w_tile_loaded[k], 16)
                if k >= 2:
                    sp.dma_start(g_tile[:, k - 2, :], g_rows[bass.ds(tile_of(c, k) * P, P), :])\
                        .then_inc(g_tile_loaded[k - 2], 16)

            produced(sp, ("gates", TB - 1))
            for m in range(NHZ):
                load_wq(m)
                if m == 1:
                    sp.dma_start(keys_sb[:, :, :], keysT).then_inc(keys_loaded, 16)
            for s in range(2):
                load_u(0, s)

            def ahead_pair(h):
                for s in range(2):
                    load_u(h + 1, s)
                    store_g(h, s)

            w_view = w_dram.rearrange("i j t -> j i t")
            for tb in range(TB):
                h0 = (AHEAD_AT[tb] - BEFORE_W[tb]) // 2
                pairs = 0
                if tb:
                    pairs = PIECES // 2
                    sp.wait_ge(w_evac, 2 + QUARTERS * WSTEPS * tb)
                    with sp.Fori(0, pairs) as i:
                        for s in range(2):
                            tiles = bass.ds((i * 2 + s) * (TILES // PIECES), TILES // PIECES)
                            load_u(i + (h0 + 1), s)
                            sp.dma_start(w_view[:, tiles, (tb - 1) * P:tb * P], wbuf[:, tiles, :])\
                                .then_inc(w_stored, 16)
                            store_g(i + h0, s)
                with sp.Fori(h0 + pairs, (AHEAD_AT[tb] + WSTEPS) // 2) as h:
                    ahead_pair(h)
            sp.wait_ge(slots_ready, TB)
            load_v(0, 0)
            load_v(0, 1)
            sp.wait_ge(w_stored, 16 * PIECES * (TB - 1))
            for s in range(2):
                sp.wait_ge(g_stored[s], 16 * (AHEAD // 2))
            sp.wait_ge(w_evac, 2 + QUARTERS * WSTEPS * TB)

            def load_step(c, last=False):
                for k in range(UNROLL):
                    if not isinstance(c, int) or c or k >= 2:
                        load_v(c, k)
                    load_w(c, k)
                    if k < 2 and not last:
                        load_u(c + AHEAD // 2 + 1, k)

            load_step(0)
            with sp.Fori(1, STEPS - 1) as c:
                load_step(c)
            load_step(STEPS - 1, last=True)
            sp.wait_ge(h_done, NHZ + TILES)
            bcast(ln2_vectors[:, 0, :], ln2_g, ln2_loaded)
            bcast(ln2_vectors[:, 1, :], ln2_b, ln2_loaded)
            for tb in range(TB):
                sp.wait_ge(ln_done, LN_2 + tb + 1)
                sp.dma_start(out[tb * P:(tb + 1) * P, :], x_sb[:, tb, :]).then_inc(stored, 16)
            sp.wait_ge(stored, 16 * TB)

        @block.tensor
        def _(pe):
            opened = [0]

            def open_job(name):
                n = JOB_AT[name]
                assert n == opened[0]
                opened[0] += 1
                if n >= BANKS:
                    evacuated(pe, JOBS[n - BANKS][0])
                return bank(name)

            def close(ins):
                ins.then_inc(pe_job, 1)

            pe.wait_ge(ident_loaded, 16)
            for tb in range(TB):
                pe.wait_ge(ln_done, LN_IN + tb + 1)
                for half in range(2):
                    ps = open_job(("xT", tb, half))
                    for j in range(4):
                        c = 4 * half + j
                        last = nc.tensor.transpose(ps[:, j * P:(j + 1) * P], x_sb[:, tb, c * P:(c + 1) * P],
                                                   ident[:, :])
                    close(last)
            evacuated(pe, ("xT", TB - 1, 1))
            passes = ((w_in_hi, x_in_hi), (w_in_hi, x_in_lo), (w_in_lo, x_in_hi))
            for m in range(CH_CHUNKS):
                ps = open_job(("hT", m))
                pe.wait_ge(w_in_lo_done, m + 1)
                piece, col = divmod(m * P, 512)
                for c in range(DC):
                    for i, (w, x) in enumerate(passes):
                        last = nc.tensor.matmul(ps[:, :], w[:, piece % 2, c, col:col + P], x[:, c, :],
                                                start=(c == 0 and i == 0), stop=(c == DC - 1 and i == 2))
                close(last)
                if m == 3:
                    pe.wait_ge(bias_loaded, 16 * (HEADS + 1))
                    for i in range(2):
                        close(nc.tensor.matmul(open_job(("bias", i)), flip, s_sb[:, i, :],
                                               start=True, stop=True))
            def scores(n):
                kind, h, qb, kbs = ATT[n]
                ps = open_job(("S", n))
                at = h if kind == "b" else C_HEAD_AT[h]
                lo = DH * (at % 2)
                qc = (BQ0 if kind == "b" else CQ0) + at // 2
                kc = BK0 + h // 2 if kind == "b" else CK0
                evacuated(pe, ("hT", qc))
                evacuated(pe, ("hT", kc))
                close(nc.tensor.matmul(ps[:, 0:P * len(kbs)], hT[lo:lo + DH, qc, qb * P:(qb + 1) * P],
                                       hT[lo:lo + DH, kc, kbs[0] * P:(kbs[-1] + 1) * P],
                                       start=True, stop=True))

            for name, piece, col, width in (("vals", 2, P, 384), ("gates", 3, 0, 512)):
                for tb in range(TB):
                    if (name, tb) == ("gates", TB - 1):
                        scores(0)
                    ps = open_job((name, tb))
                    pe.wait_ge(w_in_lo_done, 4 * (piece + 1))
                    for c in range(DC):
                        for i, (w, x) in enumerate(passes):
                            last = nc.tensor.matmul(ps[:, 0:width], x[:, c, tb * P:(tb + 1) * P],
                                                    w[:, piece % 2, c, col:col + width],
                                                    start=(c == 0 and i == 0), stop=(c == DC - 1 and i == 2))
                    close(last)

            def transposes(n):
                ps = open_job(("PT", n))
                pe.wait_ge(exp_done, n + 1)
                for j in range(len(ATT[n][3])):
                    last = nc.tensor.transpose(ps[:, j * P:(j + 1) * P], s_tile(n)[:, j * P:(j + 1) * P],
                                               ident[:, :])
                close(last)

            def values(n):
                kind, h, qb, kbs = ATT[n]
                ps = open_job(("PV", n))
                col = BV0 + DH * h if kind == "b" else CV0 + DH * (h // 2)
                evacuated(pe, ("vals", kbs[-1]))
                evacuated(pe, ("PT", n))
                for j, kb in enumerate(kbs):
                    last = nc.tensor.matmul(ps[:, 0:DH], pT_sb[:, n % 2, j * P:(j + 1) * P],
                                            ht[:, kb, col:col + DH], start=(j == 0), stop=(j == len(kbs) - 1))
                close(last)

            for n in range(NATT + 3):
                if 1 <= n < NATT:
                    scores(n)
                if 2 <= n < NATT + 2:
                    transposes(n - 2)
                if n >= 3:
                    values(n - 3)
            for c in range(2):
                ps = open_job(("pool", c))
                pe.wait_ge(pooled, c + 1)
                for g in range(2):
                    lo = DH * g
                    last = nc.tensor.matmul(ps[lo:lo + DH, :], pool_lin_sb[lo:lo + DH, c, :],
                                            hT[lo:lo + DH, A0 + c, :], start=True, stop=True)
                close(last)
            pe.wait_ge(masks_set, 2)
            for tb in range(TB):
                ps = open_job(("sgu", tb))
                pe.wait_ge(ln_done, LN_SGU + tb + 1)
                for g in range(HEADS):
                    last = nc.tensor.matmul(ps[:, g * DH:(g + 1) * DH], sgu_w_sb[:, g, :],
                                            ht[:, tb, DV0 + g * DH:DV0 + (g + 1) * DH], start=True, stop=True)
                close(last)
            for c in range(6):
                ps = open_job(("mixT", c))
                evacuated(pe, ("PV", NATT - 1) if c < 4 else ("sgu", TB - 1))
                for tb in range(TB):
                    src = mix_tok[:, tb, c * P:(c + 1) * P] if c < 4 else \
                        ht[:, tb, DU0 + (c - 4) * P:DU0 + (c - 3) * P]
                    last = nc.tensor.transpose(ps[:, tb * P:(tb + 1) * P], src, ident[:, :])
                close(last)
            pe.wait_ge(w_out_loaded, 16)
            for what, tb in OUT_ORDER:
                if what == "x1T":
                    pe.wait_ge(ln_done, LN_1 + tb + 1)
                for half in range(2):
                    ps = open_job((what, tb, half))
                    if what == "out":
                        for c in range(DC):
                            evacuated(pe, ("pool", c) if c < 2 else ("mixT", c - 2))
                            last = nc.tensor.matmul(ps[:, :], mixT[:, c, tb * P:(tb + 1) * P],
                                                    w_out_sb[:, c, half * 512:(half + 1) * 512],
                                                    start=(c == 0), stop=(c == DC - 1))
                    else:
                        for j in range(4):
                            c = 4 * half + j
                            last = nc.tensor.transpose(ps[:, j * P:(j + 1) * P],
                                                       x_sb[:, tb, c * P:(c + 1) * P], ident[:, :])
                    close(last)
            pe.sem_inc(w_product, QUARTERS)

            def transpose_slots(tb):
                pe.wait_ge(slots_ready, tb + 1)
                need(pe, slots_evac, tb)
                for i in range(3):
                    last = nc.tensor.transpose(psum[:, SLOTS_BANK, i * P:(i + 1) * P], slots[:, i, :], ident[:, :])
                last.then_inc(slots_transposed, 1)

            def hidden_part(h, s, part, before=NHZ):
                if part == 0:
                    n = h * 2 + (s + before)
                    need(pe, h_taken, n - 1)
                    pe.wait_ge(u_hi_done, n + 1)
                    pe.wait_ge(u_lo_done, n + 1)
                for d in (2 * part, 2 * part + 1):
                    for w, x, i in ((u_hi, x_hi, 0), (u_hi, x_lo, 1), (u_lo, x_hi, 2)):
                        last = nc.tensor.matmul(psum[:, s, :], w[:, s, d, :], x[:, d, :],
                                                start=(d == 0 and i == 0), stop=(d == DC - 1 and i == 2))
                if part == 3:
                    last.then_inc(h_done, 1)

            def hidden(h, s, before=NHZ):
                for part in range(4):
                    hidden_part(h, s, part, before)

            def key_scores(m):
                pe.wait_ge(h_taken, m + 1)
                need(pe, sc_evac, m - 1)
                for tb in range(TB):
                    last = nc.tensor.matmul(psum[:, 2 + m % 2, tb * P:(tb + 1) * P],
                                            q_sb[:, m % 2, tb * P:(tb + 1) * P], keys_sb[:, m, :],
                                            start=True, stop=True)
                last.then_inc(sc_done, 1)

            def products_of_w(tb):
                with pe.Fori(0, WSTEPS // 2) as g:
                    for s in range(2):
                        for q in range(QUARTERS):
                            turn = g * 2 + (s + tb * WSTEPS)
                            done = turn * QUARTERS + q
                            pe.wait_ge(l_built, (done + 1) * 4)
                            pe.wait_ge(r_built, done + 1)
                            pe.wait_ge(w_evac, done + 1)
                            for i in range(4):
                                last = nc.tensor.matmul(psum[:, BANKS + q % 2, i * P:(i + 1) * P],
                                                        l_ring[:, 4 * q + i, :], r_ring[:, 4 * q + i, :],
                                                        start=True, stop=True)
                            last.then_inc(w_product, 1)
                            hidden_part(g + AHEAD_AT[tb] // 2, s, q)

            evacuated(pe, ("mixT", 5))
            evacuated(pe, ("x1T", TB - 1, 1))
            pe.wait_ge(keys_loaded, 16)
            for m in range(NHZ):
                hidden(m // 2, m % 2, before=0)
                if m:
                    key_scores(m - 1)
            key_scores(NHZ - 1)
            for tb in range(TB):
                with pe.Fori((AHEAD_AT[tb] - BEFORE_W[tb]) // 2, AHEAD_AT[tb] // 2 - 1) as h:
                    for s in range(2):
                        hidden(h, s)
                hidden(AHEAD_AT[tb] // 2 - 1, 0)
                transpose_slots(tb)
                hidden(AHEAD_AT[tb] // 2 - 1, 1)
                products_of_w(tb)

            pe.wait_ge(slots_evac, TB)
            pe.wait_ge(w_evac, 2 + QUARTERS * WSTEPS * TB)

            def add_up(c, pair, part):
                n = c * UNROLL + 2 * pair
                if part == 0:
                    for s in (v_hi_done, v_lo_done, a_hi_done, a_lo_done):
                        pe.wait_ge(s, n + 2)
                for q in range(4):
                    job = (c * 2 + pair) * GROUP_JOBS + 4 * part + q
                    need(pe, y_evac, job - 3)
                    tb, half = divmod(4 * part + q, 2)
                    passes = [(a, v, 2 * pair + t) for t in range(2)
                              for a, v in ((a_hi, v_hi), (a_hi, v_lo), (a_lo, v_hi))]
                    for i, (a, v, t) in enumerate(passes):
                        last = nc.tensor.matmul(psum[:, 4 + q, :], a[:, t, tb * P:(tb + 1) * P],
                                                v[:, t, half * 512:(half + 1) * 512],
                                                start=(i == 0), stop=(i == len(passes) - 1))
                    last.then_inc(y_done, 1)

            def step(c, first=False):
                for k in range(2):
                    hidden(c + AHEAD // 2, k)
                    if not first:
                        add_up(c - 1, 1, k)
                add_up(c, 0, 0)
                add_up(c, 0, 1)

            step(0, first=True)
            with pe.Fori(1, STEPS) as c:
                step(c)
            add_up(STEPS - 1, 1, 0)
            add_up(STEPS - 1, 1, 1)

        @block.scalar
        def _(act):
            def evac(name, out_ap, in_ap, func=ACT.Copy, **kw):
                produced(act, name)
                nc.scalar.activation(out_ap, in_ap, func, **kw).then_inc(act_evac, 1)

            def ln_std(n):
                act.wait_ge(var_ready, n + 1)
                nc.scalar.activation(std[:, 0:1], mean_var[:, 1:2], ACT.Sqrt, bias=eps[:, :]).then_inc(std_ready, 1)

            act.wait_ge(eps_set, 1)
            ln_std(LN_IN)
            def high_w_in(m):
                piece, col = divmod(m * P, 512)
                act.wait_ge(w_in_loaded[piece], 16)
                if piece >= 2 and col == 0:
                    produced(act, ("hT", 4 * (piece - 1) - 1))
                nc.scalar.activation(w_in_hi[:, piece % 2, :, col:col + P],
                                     w_in_raw[:, piece % 2, :, col:col + P], ACT.Copy).then_inc(w_in_hi_done, 1)

            for tb in range(TB):
                if tb + 1 < TB:
                    ln_std(LN_IN + tb + 1)
                for half in range(2):
                    produced(act, ("xT", tb, half))
                    nc.scalar.activation(x_in_hi[:, 4 * half:4 * half + 4, tb * P:(tb + 1) * P],
                                         bank(("xT", tb, half)).rearrange("p (j t) -> p j t", j=4), ACT.Copy)\
                        .then_inc(x_in_hi_done, 1)
                if tb >= 2:
                    high_w_in(tb - 2)
            high_w_in(2)
            for m in range(1, CH_CHUNKS, 2):
                for k in (m + 2, m + 3):
                    high_w_in(k)
                evac(("hT", m), hT[:, m, :], bank(("hT", m)))
            for m in range(CH_CHUNKS + 2, 2 * DC):
                high_w_in(m)
            def exponentials(n):
                kind, h, qb, kbs = ATT[n]
                act.wait_ge(max_ready, n + 1)
                s = s_tile(n)[:, 0:P * len(kbs)]
                r = row[:, n % 8, :]
                if kind == "c":
                    nc.scalar.activation(small[:, n % 8:n % 8 + 1], sink_sb[:, h:h + 1], ACT.Exp,
                                         bias=r[:, 1:2]).then_inc(sink_exp_done, 1)
                nc.scalar.activation(s, s, ACT.Exp, bias=r[:, 1:2], accum_out=r[:, 2:3]).then_inc(exp_done, 1)

            for tb in range(TB):
                if tb == TB - 1:
                    exponentials(0)
                evac(("gates", tb), ht[:, tb, DU0:TOKW], bank(("gates", tb)), ACT.Gelu)
                if tb < TB - 1:
                    ln_std(LN_SGU + tb)
            for n in range(NATT + 2):
                if 1 <= n < NATT:
                    exponentials(n)
                if n >= 2:
                    m = n - 2
                    if m >= 2:
                        produced(act, ("PV", m - 2))
                    w = P * len(ATT[m][3])
                    evac(("PT", m), pT_sb[:, m % 2, 0:w], bank(("PT", m))[:, 0:w])
            ln_std(LN_SGU + TB - 1)
            for c in range(2):
                evac(("pool", c), mixT[:, c, :], bank(("pool", c)), scale=pool_scale_sb[:, c:c + 1])
            for c in range(6):
                evac(("mixT", c), mixT[:, 2 + c, :], bank(("mixT", c)))
            def u_high(h, s, before=NHZ):
                act.wait_ge(u_raw_loaded[s], (h + (before // 2 + 1)) * 16)
                need(act, h_done, h * 2 + (s + before - 1))
                nc.scalar.activation(u_hi[:, s, :, :], u_raw[:, s, :, :], ACT.Copy).then_inc(u_hi_done, 1)

            for s in range(2):
                u_high(0, s, before=0)
            ln_std(LN_1)
            for tb in range(TB):
                if tb + 1 < TB:
                    ln_std(LN_1 + tb + 1)
                for half in range(2):
                    produced(act, ("x1T", tb, half))
                    nc.scalar.activation(x_hi[:, 4 * half:4 * half + 4, tb * P:(tb + 1) * P],
                                         bank(("x1T", tb, half)).rearrange("p (j t) -> p j t", j=4), ACT.Copy)\
                        .then_inc(x_hi_done, 1)
            act.sem_inc(w_evac, 2)

            def after_h(h, s):
                act.wait_ge(h_done, h * 2 + (s + NHZ + 1))
                need(act, g_stored[s], h * 16)
                nc.scalar.activation(g_stage[:, s, :], psum[:, s, :], ACT.Gelu).then_inc(h_taken, 1)
                u_high(h + 1, s)

            def block_of_w(b):
                if b:
                    act.wait_ge(w_stored, 16 * PIECES * b)
                with act.Fori(0, WSTEPS // 2) as g:
                    def evacuate(s, q):
                        act.wait_ge(w_product, (g * 2 + (s + b * WSTEPS)) * QUARTERS + (q + 1 + QUARTERS))
                        act.sem_inc(w_turn, 1)
                        nc.scalar.activation(
                            wbuf[:, :, bass.ds(g * (2 * TOKENS) + (s * TOKENS + 4 * q), 4)]
                            .rearrange("p i t -> p t i"),
                            psum[:, BANKS + q % 2, :].rearrange("p (t i) -> p t i", t=4), ACT.Copy)\
                            .then_inc(w_evac, 1)

                    for s in range(2):
                        after_h(g + (AHEAD_AT[b] // 2 - 1 + s), 1 - s)
                        for q in range(QUARTERS):
                            evacuate(s, q)
            def gates_exp(tb):
                act.wait_ge(gate_in, tb + 1)
                nc.scalar.activation(slots[:, 2, :], slots[:, 2, :], ACT.Exp).then_inc(gate_exp, 1)

            for m in range(NHZ):
                act.wait_ge(h_done, m + 1)
                need(act, sc_done, m - 1)
                nc.scalar.activation(q_sb[:, m % 2, :], psum[:, m % 2, :], ACT.Copy).then_inc(h_taken, 1)
                u_high((m + 2) // 2, m % 2, before=0)

            def evacuate_slots(tb):
                act.wait_ge(slots_transposed, tb + 1)
                if tb:
                    act.wait_ge(l_built, P * tb)
                    act.wait_ge(r_built, QUARTERS * WSTEPS * tb)
                nc.scalar.activation(slotT[:, :, :],
                                     psum[:, SLOTS_BANK, 0:3 * P].rearrange("p (i t) -> p i t", i=3), ACT.Copy)\
                    .then_inc(slots_evac, 1)

            for tb in range(TB):
                h = AHEAD_AT[tb] // 2 - 1
                if tb == 0:
                    after_h(0, 0)
                    for i in range(1, h):
                        after_h(i - 1, 1)
                        after_h(i, 0)
                else:
                    with act.Fori((AHEAD_AT[tb] - BEFORE_W[tb]) // 2, h) as i:
                        after_h(i - 1, 1)
                        after_h(i, 0)
                after_h(h - 1, 1)
                gates_exp(tb)
                evacuate_slots(tb)
                after_h(h, 0)
                block_of_w(tb)
            after_h(AHEAD // 2 - 1, 1)

            def step(c, last=False):
                for k in range(2):
                    v_high(c, k)
                for k in range(2):
                    n = c * 2 + (AHEAD + k)
                    act.wait_ge(h_done, n + (NHZ + 1))
                    need(act, a_lo_done, c * UNROLL + k - 1)
                    nc.scalar.activation(a_full[:, k, :], psum[:, k, :], ACT.Gelu).then_inc(h_taken, 1)
                    if not last:
                        u_high(c + (AHEAD // 2 + 1), k)
                    a_high(c, k)
                for k in range(2, UNROLL):
                    a_high(c, k)
                    v_high(c, k)

            def v_high(c, k):
                act.wait_ge(v_raw_loaded[k % 2], (c * 2 + (k // 2 + 1)) * 16)
                need(act, y_done, ((c - 1) * 2 + (k // 2 + 1)) * GROUP_JOBS)
                nc.scalar.activation(v_hi[:, k, :], v_raw[:, k % 2, :], ACT.Copy).then_inc(v_hi_done, 1)

            def a_high(c, k):
                act.wait_ge(a_done, c * UNROLL + (k + 1))
                need(act, y_done, ((c - 1) * 2 + (k // 2 + 1)) * GROUP_JOBS)
                nc.scalar.activation(a_hi[:, k, :], a_full[:, k % 2, :], ACT.Copy).then_inc(a_hi_done, 1)

            step(0)
            with act.Fori(1, STEPS - 1) as c:
                step(c)
            step(STEPS - 1, last=True)
            for tb in range(TB):
                ln_std(LN_2 + tb)

        @block.vector
        def _(dve):
            steps = [0]

            def link(ins):
                steps[0] += 1
                ins.then_inc(dve_chain, 1)
                dve.wait_ge(dve_chain, steps[0])

            def evac_done(ins):
                ins.then_inc(dve_evac, 1)

            def layer_norm(n, src, width, gain, bias):
                pieces = max(1, width // 512)
                w = width // pieces
                for i in range(pieces):
                    last = nc.vector.bn_stats(stats[:, i, :], src[:, i * w:(i + 1) * w])
                link(last)
                nc.vector.bn_aggr(mean_var[:, :], stats[:, 0:pieces, :].rearrange("p a b -> p (a b)"))\
                    .then_inc(var_ready, 1)
                dve.wait_ge(var_ready, n + 1)
                nc.vector.scalar_tensor_tensor(out=src, in0=src, scalar=mean_var[:, 0:1], in1=gain,
                                               op0=ALU.subtract, op1=ALU.mult)
                dve.wait_ge(std_ready, n + 1)
                link(nc.vector.reciprocal(std[:, 1:2], std[:, 0:1]))
                nc.vector.scalar_tensor_tensor(out=src, in0=src, scalar=std[:, 1:2], in1=bias,
                                               op0=ALU.mult, op1=ALU.add).then_inc(ln_done, 1)

            def low_x_in(tb):
                for half in range(2):
                    dve.wait_ge(x_in_hi_done, 2 * tb + half + 1)
                    chunks = slice(4 * half, 4 * half + 4)
                    high = x_in_hi[:, chunks, tb * P:(tb + 1) * P].bitcast(F32)
                    evac_done(nc.vector.tensor_tensor(
                        x_in_lo[:, chunks, tb * P:(tb + 1) * P],
                        bank(("xT", tb, half)).rearrange("p (j t) -> p j t", j=4), high, ALU.subtract))

            dve.wait_ge(ln_in_loaded, 32)
            for tb in range(TB):
                dve.wait_ge(x_loaded[tb], 16)
                layer_norm(LN_IN + tb, x_sb[:, tb, :], D, lnv[0], lnv[1])
                if tb:
                    low_x_in(tb - 1)
            low_x_in(TB - 1)

            def sgu_norm(tb):
                evacuated(dve, ("gates", tb))
                layer_norm(LN_SGU + tb, ht[:, tb, DV0:DV0 + GROUP], GROUP, lnv_sgu[:, 0, :], lnv_sgu[:, 1, :])

            def pool_means():
                evacuated(dve, ("hT", A0 + 1))
                for c in range(2):
                    a = hT[:, A0 + c, :]
                    src = a
                    for k in range(4 if c else 2):
                        shift = 1 << k
                        lo = DH if k == (3 if c else 1) else 0
                        dst = s_sb[:, k % 2, :]
                        if lo and k:
                            nc.vector.tensor_copy(dst[0:lo, :], src[0:lo, :])
                        nc.vector.tensor_copy(dst[lo:P, 0:shift], src[lo:P, 0:shift])
                        link(nc.vector.tensor_tensor(dst[lo:P, shift:T], src[lo:P, shift:T],
                                                     src[lo:P, 0:T - shift], ALU.add))
                        src = dst
                    link(nc.vector.tensor_tensor(small[:, 0:16], src[:, 0:16], inv_count[:, c, :], ALU.mult))
                    link(nc.vector.tensor_tensor(small[:, 0:16], small[:, 0:16], a[:, 0:16], ALU.subtract))
                    for g in range(2):
                        lo = DH * g
                        w = POOL_WINDOWS[2 * c + g]
                        last = nc.vector.scalar_tensor_tensor(out=a[lo:lo + DH, 16:T], in0=src[lo:lo + DH, 16:T],
                                                              scalar=1.0 / w, in1=a[lo:lo + DH, 16:T],
                                                              op0=ALU.mult, op1=ALU.subtract)
                    link(last)
                    nc.vector.tensor_copy(a[:, 0:16], small[:, 0:16]).then_inc(pooled, 1)
                    dve.wait_ge(pooled, c + 1)

            for m in range(0, CH_CHUNKS, 2):
                produced(dve, ("hT", m))
                evac_done(nc.vector.tensor_copy(hT[:, m, :], bank(("hT", m))))
                if m == 2:
                    for i in range(2):
                        produced(dve, ("bias", i))
                        evac_done(nc.vector.tensor_copy(bias_b[:, 2 * i:2 * i + 2, :],
                                                        bank(("bias", i)).rearrange("p (h n) -> p h n", h=2)))
            def biased_scores(n):
                kind, h, qb, kbs = ATT[n]
                ps = bank(("S", n))
                produced(dve, ("S", n))
                if n >= 4:
                    produced(dve, ("PT", n - 4))
                s = s_tile(n)
                r = row[:, n % 8, :]
                near = min(2, len(kbs))
                far = P * (len(kbs) - near)
                bias = bias_b if kind == "b" else alibi
                if far:
                    nc.vector.tensor_scalar(s[:, 0:far], ps[:, 0:far], SCALE, bias_b[:, h, 0:1],
                                            ALU.mult, ALU.add)
                last = nc.vector.scalar_tensor_tensor(
                    out=s[:, far:far + P * near], in0=ps[:, far:far + P * near], scalar=SCALE,
                    in1=bias[:, h, 256 - P * near:256], op0=ALU.mult, op1=ALU.add)
                evac_done(last)
                dve.wait_ge(dve_evac, evacuations(JOB_AT[("S", n)] + 1)["dve"])
                link(nc.vector.reduce_max(r[:, 0:1], s[:, 0:far + P * near], AX.X))
                if kind == "c":
                    link(nc.vector.tensor_tensor(r[:, 0:1], r[:, 0:1], sink_sb[:, h:h + 1], ALU.max))
                nc.vector.tensor_scalar(r[:, 1:2], r[:, 0:1], -1.0, None, ALU.mult).then_inc(max_ready, 1)

            dve.wait_ge(tables_loaded, 16 * N_TABLES)
            pool_means()
            dve.wait_ge(sgu_w_loaded, 48)
            for tb in range(TB):
                produced(dve, ("vals", tb))
                evac_done(nc.vector.tensor_copy(ht[:, tb, 0:384], bank(("vals", tb))[:, 0:384]))
            for tb in range(TB - 1):
                sgu_norm(tb)
            dve.wait_ge(masks_set, 2)
            biased_scores(0)

            dve.wait_ge(alibi_loaded, 16)
            cs = 0
            for n in range(NATT + 3):
                if 1 <= n < NATT:
                    biased_scores(n)
                if n >= 3:
                    m = n - 3
                    kind, h, qb, kbs = ATT[m]
                    r = row[:, m % 8, :]
                    dve.wait_ge(exp_done, m + 1)
                    if kind == "c":
                        cs += 1
                        dve.wait_ge(sink_exp_done, cs)
                        link(nc.vector.tensor_tensor(r[:, 2:3], r[:, 2:3], small[:, m % 8:m % 8 + 1], ALU.add))
                    link(nc.vector.reciprocal(r[:, 3:4], r[:, 2:3]))
                    produced(dve, ("PV", m))
                    col = (0 if kind == "b" else GROUP) + DH * h
                    evac_done(nc.vector.tensor_scalar(mix_tok[:, qb, col:col + DH], bank(("PV", m))[:, 0:DH],
                                                      r[:, 3:4], None, ALU.mult))
            sgu_norm(TB - 1)
            for tb in range(TB):
                produced(dve, ("sgu", tb))
                for g in range(HEADS):
                    last = nc.vector.scalar_tensor_tensor(
                        out=ht[:, tb, DU0 + g * DH:DU0 + (g + 1) * DH],
                        in0=bank(("sgu", tb))[:, g * DH:(g + 1) * DH], scalar=sgu_b_sb[:, g:g + 1],
                        in1=ht[:, tb, DU0 + g * DH:DU0 + (g + 1) * DH], op0=ALU.add, op1=ALU.mult)
                evac_done(last)
            for what, tb in OUT_ORDER:
                for half in range(2):
                    if what == "out":
                        produced(dve, ("out", tb, half))
                        cols = slice(half * 512, (half + 1) * 512)
                        evac_done(nc.vector.scalar_tensor_tensor(
                            out=x_sb[:, tb, cols], in0=x_sb[:, tb, cols], scalar=ALPHA,
                            in1=bank(("out", tb, half)), op0=ALU.mult, op1=ALU.add))
                    else:
                        dve.wait_ge(x_hi_done, 2 * tb + half + 1)
                        chunks = slice(4 * half, 4 * half + 4)
                        evac_done(nc.vector.tensor_tensor(
                            x_lo[:, chunks, tb * P:(tb + 1) * P],
                            bank(("x1T", tb, half)).rearrange("p (j t) -> p j t", j=4),
                            x_hi[:, chunks, tb * P:(tb + 1) * P].bitcast(F32), ALU.subtract))
                if what == "out":
                    evacuated(dve, ("out", tb, 1))
                    layer_norm(LN_1 + tb, x_sb[:, tb, :], D, lnv[2], lnv[3])

            def top16(rows, evacuates=0):
                for values, _, scores, _ in rows:
                    last = nc.vector.max(values[:, 0:8], scores)
                link(last)
                for values, indices, scores, scratch in rows:
                    nc.vector.max_index(indices[:, 0:8], values[:, 0:8], scores)
                    last = nc.vector.match_replace(scratch, values[:, 0:8], scores, LOWEST)
                if evacuates:
                    last.then_inc(sc_evac, 1)
                    dve.wait_ge(sc_evac, evacuates)
                else:
                    link(last)
                for values, _, _, scratch in rows:
                    last = nc.vector.max(values[:, 8:16], scratch)
                link(last)
                for values, indices, _, scratch in rows:
                    last = nc.vector.max_index(indices[:, 8:16], values[:, 8:16], scratch)
                link(last)

            def best_pairs(tb, heads):
                own = slice(heads[0], heads[-1] + 1)
                tv = topv_all[:, tb, :].rearrange("p (h z k) -> p h z k", h=PH, z=2)
                c4 = cand.rearrange("p (h a b) -> p h a b", h=PH, a=TOPK)
                shape = [P, len(heads), TOPK, TOPK]
                link(nc.vector.tensor_tensor(c4[:, own, :, :], tv[:, own, 0, :].unsqueeze(3).to_broadcast(shape),
                                             tv[:, own, 1, :].unsqueeze(2).to_broadcast(shape), ALU.add))
                top16([(best[:, 16 * h:16 * h + 16], pos[:, 16 * h:16 * h + 16],
                        cand[:, 256 * h:256 * h + 256], work[:, 256 * i:256 * i + 256])
                       for i, h in enumerate(heads)])

            for m in range(NHZ):
                dve.wait_ge(sc_done, m + 1)
                own = slice(TOPK * m, TOPK * (m + 1))
                top16([(topv_all[:, tb, own], topi_all[:, tb, own],
                        psum[:, 2 + m % 2, tb * P:(tb + 1) * P], work[:, tb * P:(tb + 1) * P])
                       for tb in range(TB)], m + 1)
                if m % 2:
                    best_pairs(0, [m // 2])

            def route_block(tb):
                if tb:
                    dve.wait_ge(w_product, QUARTERS * (WSTEPS * tb + 1))
                    for pair in range(PH // 2):
                        best_pairs(tb, [2 * pair, 2 * pair + 1])
                tf = topi_f.rearrange("p (h z k) -> p h z k", h=PH, z=2)
                link(nc.vector.tensor_copy(topi_f, topi_all[:, tb, :]))
                shape = [P, PH, TOPK, TOPK]
                for z, where in enumerate((pos_a, pos_b)):
                    op, n = ((ALU.logical_shift_right, 4), (ALU.bitwise_and, 15))[z]
                    link(nc.vector.tensor_scalar(where, pos, n, None, op))
                if tb:
                    dve.wait_ge(slots_transposed, tb)
                hot4 = hot.rearrange("p (h k a) -> p h k a", h=PH, k=TOPK)
                hot3 = hot.rearrange("p (s a) -> p s a", a=TOPK)
                for z, where in enumerate((pos_a, pos_b)):
                    key = slots[:, z, :]
                    link(nc.vector.tensor_copy(key, where))
                    link(nc.vector.tensor_tensor(hot3, key.unsqueeze(2).to_broadcast([P, NSEL, TOPK]),
                                                 iota[:, 0:TOPK].unsqueeze(1).to_broadcast([P, NSEL, TOPK]),
                                                 ALU.is_equal))
                    link(nc.vector.tensor_tensor(hot4, hot4, tf[:, :, z, :].unsqueeze(2).to_broadcast(shape),
                                                 ALU.mult))
                    link(nc.vector.tensor_reduce(key, hot3, AX.X, ALU.add))
                g3 = slots[:, 2, :].rearrange("p (h k) -> p h k", h=PH)
                b3 = best.rearrange("p (h k) -> p h k", h=PH)
                nc.vector.tensor_tensor(g3, b3, b3[:, :, 0:1].to_broadcast([P, PH, TOPK]), ALU.subtract)\
                    .then_inc(gate_in, 1)
                dve.wait_ge(gate_exp, tb + 1)
                link(nc.vector.tensor_reduce(small[:, 0:PH], g3, AX.X, ALU.add))
                link(nc.vector.reciprocal(small[:, 8:8 + PH], small[:, 0:PH]))
                nc.vector.tensor_tensor(g3, g3, small[:, 8:8 + PH].unsqueeze(2).to_broadcast([P, PH, TOPK]),
                                        ALU.mult).then_inc(slots_ready, 1)

            def gate_rows(b):
                dve.wait_ge(slots_evac, b + 1)
                with dve.Fori(0, WSTEPS) as g:
                    for k in range(TOKENS):
                        if k % 4 == 0:
                            dve.wait_ge(w_product, (g + b * WSTEPS) * QUARTERS + (k // 4 + 1))
                        nc.vector.tensor_scalar(l_ring[:, k, :], iota[:, :],
                                                slotT[:, 1, bass.ds(g * TOKENS + k, 1)],
                                                slotT[:, 2, bass.ds(g * TOKENS + k, 1)],
                                                ALU.is_equal, ALU.mult).then_inc(l_built, 1)
                        if k % 4 == 3:
                            shape = [P, 4, P]
                            first = slotT[:, 0, bass.ds(g * TOKENS + (k - 3), 4)]
                            nc.vector.tensor_tensor(r_ring[:, k - 3:k + 1, :],
                                                    iota[:, :].unsqueeze(1).to_broadcast(shape),
                                                    first.unsqueeze(2).to_broadcast(shape),
                                                    ALU.is_equal).then_inc(r_built, 1)

            for tb in range(TB):
                route_block(tb)
                gate_rows(tb)

            for tb in range(TB):
                produced(dve, ("x1T", tb, 1))
                last = nc.vector.tensor_scalar(x_sb[:, tb, :], x_sb[:, tb, :], ALPHA, None, ALU.mult)
            link(last)

            def make_a(c, k):
                n = c * UNROLL + k
                dve.wait_ge(w_tile_loaded[k], (c + 1) * 16)
                a = a_full[:, k % 2, :]
                if k < 2:
                    dve.wait_ge(h_taken, c * 2 + (NHZ + AHEAD + k + 1))
                    g = a
                else:
                    dve.wait_ge(g_tile_loaded[k - 2], (c + 1) * 16)
                    g = g_tile[:, k - 2, :]
                nc.vector.tensor_tensor(a[:, 0:T - P], w_tile[:, k, :], g[:, 0:T - P], ALU.mult)
                last_block = wbuf[:, bass.ds(tile_of(c, k), 1), :].rearrange("p i t -> p (i t)")
                nc.vector.tensor_tensor(a[:, T - P:T], last_block, g[:, T - P:T], ALU.mult).then_inc(a_done, 1)
                dve.wait_ge(a_hi_done, n + 1)
                nc.vector.tensor_tensor(a_lo[:, k, :], a_full[:, k % 2, :], a_hi[:, k, :].bitcast(F32),
                                        ALU.subtract).then_inc(a_lo_done, 1)

            def add_y(c, pair, jobs):
                for i in jobs:
                    job = (c * 2 + pair) * GROUP_JOBS + i
                    tb, half = divmod(i, 2)
                    y = x_sb[:, tb, half * 512:(half + 1) * 512]
                    need(dve, y_evac, job - GROUP_JOBS + 1)
                    dve.wait_ge(y_done, job + 1)
                    nc.vector.tensor_tensor(y, y, psum[:, 4 + i % 4, :], ALU.add).then_inc(y_evac, 1)

            def step(c, first=False):
                halves = (range(4), range(4, 8))
                for k in range(2):
                    make_a(c, k)
                    if not first:
                        add_y(c - 1, 1, halves[k])
                for k in range(2):
                    make_a(c, 2 + k)
                    add_y(c, 0, halves[k])

            step(0, first=True)
            with dve.Fori(1, STEPS) as c:
                step(c)
            dve.wait_ge(ln2_loaded, 32)
            for tb in range(TB):
                add_y(STEPS - 1, 1, (2 * tb, 2 * tb + 1))
                dve.wait_ge(y_evac, 2 * STEPS * GROUP_JOBS - 2 * (TB - 1 - tb))
                layer_norm(LN_2 + tb, x_sb[:, tb, :], D, ln2_vectors[:, 0, :], ln2_vectors[:, 1, :])

        @block.gpsimd
        def _(pool):
            nc.gpsimd.memset(eps[:, :], EPS).then_inc(eps_set, 1)
            for m in range(2 * DC):
                piece, col = divmod(m * P, 512)
                pool.wait_ge(w_in_hi_done, m + 1)
                nc.gpsimd.tensor_tensor(w_in_lo[:, piece % 2, :, col:col + P],
                                        w_in_raw[:, piece % 2, :, col:col + P],
                                        w_in_hi[:, piece % 2, :, col:col + P].bitcast(F32), ALU.subtract)\
                    .then_inc(w_in_lo_done, 1)
            pool.wait_ge(sgu_w_loaded, 48)
            nc.gpsimd.affine_select(out=sgu_w_sb, in_=sgu_w_sb, compare_op=ALU.is_ge, fill=0.0,
                                    base=0, pattern=[[0, HEADS], [1, P]], channel_multiplier=-1)\
                .then_inc(masks_set, 1)
            evacuated(pool, ("bias", 1))
            nc.gpsimd.memset(bias_b[0:CHUNK, :, 256 - CHUNK:256], NEG).then_inc(masks_set, 1)
            def u_low(h, s, before=NHZ):
                pool.wait_ge(u_hi_done, h * 2 + (s + before + 1))
                nc.gpsimd.tensor_tensor(u_lo[:, s, :, :], u_raw[:, s, :, :], u_hi[:, s, :, :].bitcast(F32),
                                        ALU.subtract).then_inc(u_lo_done, 1)

            for m in range(NHZ):
                u_low(m // 2, m % 2, before=0)
            u_low(0, 0)
            with pool.Fori(0, AHEAD // 2) as h:
                u_low(h, 1)
                u_low(h + 1, 0)
            u_low(AHEAD // 2, 1)

            def v_low(c, k):
                pool.wait_ge(v_hi_done, c * UNROLL + (k + 1))
                nc.gpsimd.tensor_tensor(v_lo[:, k, :], v_raw[:, k % 2, :], v_hi[:, k, :].bitcast(F32),
                                        ALU.subtract).then_inc(v_lo_done, 1)

            def step(c, last=False):
                for k in range(UNROLL):
                    if k == 2 and not last:
                        for s in range(2):
                            u_low(c + (AHEAD // 2 + 1), s)
                    v_low(c, k)

            for s in range(2):
                pool.wait_ge(g_stored[s], 16 * (AHEAD // 2))
            with pool.Fori(0, STEPS - 1) as c:
                step(c)
            step(STEPS - 1, last=True)


def shape_constants():
    i = np.arange(P)[:, None]
    u = np.arange(2 * P)[None, :]
    dist = np.abs(P + i - u).astype(np.float32)
    key_chunk = u // CHUNK
    own = 2 + i // CHUNK
    seen = (key_chunk == own) | (key_chunk == own - 1)
    slopes = 2.0 ** (-8.0 * (np.arange(HEADS, dtype=np.float32) + 1.0) / HEADS)
    alibi = np.where(seen[:, None, :], -slopes[None, :, None] * dist[:, None, :], NEG).astype(np.float32)
    inv = np.zeros((P, 2, 16), np.float32)
    for g, w in enumerate(POOL_WINDOWS):
        inv[DH * (g % 2):DH * (g % 2) + DH, g // 2, :] = 1.0 / np.minimum(np.arange(16) + 1, w)
    iota = np.tile(np.arange(P, dtype=np.float32), (P, 1))
    return np.eye(P, dtype=np.float32), alibi, inv, iota


def kernel(**inputs):
    import concourse.bacc as bacc
    from concourse.bass_utils import run_bass_kernel_spmd

    a = {k: np.asarray(v) for k, v in inputs.items()}
    w_in = a["w_in"][0]
    cq = [1024 + DH * h + np.arange(DH) for h in C_HEAD_AT]
    order = np.concatenate([np.arange(0, 768), *cq, np.arange(1280, 1408),
                            np.arange(768, 1024), np.arange(1408, 1536), np.arange(1536, 2048)])
    rel_at = np.clip(256 - np.arange(512), -REL_CLIP, REL_CLIP) + REL_CLIP
    ident, alibi, inv, iota = shape_constants()
    arrays = {
        "x": a["x"].reshape(T, D),
        "w_in": w_in[:, order],
        "w_out": a["w_out"][0],
        "pool_lin": a["pool_lin"][0].reshape(2, 2, DH, DH).transpose(1, 2, 0, 3).reshape(P, 2, DH),
        "pool_scale": a["pool_scale"][0].reshape(2, P).T,
        "rel_ext": a["rel_bias"][0][:, rel_at],
        "sinks": a["sinks"][0],
        "sgu_ln_g": a["sgu_ln_g"][0],
        "sgu_ln_b": a["sgu_ln_b"][0],
        "sgu_wT": a["sgu_w"][0].transpose(2, 0, 1),
        "sgu_bT": a["sgu_b"][0].T,
        "ln_in_g": a["ln_in_g"], "ln_in_b": a["ln_in_b"],
        "ln1_g": a["ln1_g"][0], "ln1_b": a["ln1_b"][0],
        "ln2_g": a["ln2_g"][0], "ln2_b": a["ln2_b"][0],
        "wqT": a["peer_wq"][0].reshape(DC, P, NHZ, P).transpose(2, 1, 0, 3).reshape(NHZ * P, D),
        "keysT": a["peer_keys"][0].reshape(NHZ, NKEYS, P).transpose(2, 0, 1),
        "expert_uT": a["expert_u"][0].reshape(TILES, P, DC, P).transpose(0, 3, 2, 1).reshape(TILES * P, D),
        "expert_v": a["expert_v"][0],
        "identity_c": ident, "flip_c": ident[::-1], "alibi_c": alibi, "inv_count_c": inv, "iota_c": iota,
    }
    nc = bacc.Bacc("TRN2", target_bir_lowering=False, num_devices=1)
    arrays = {f"in_{k}": np.ascontiguousarray(v) for k, v in arrays.items()}
    args = [nc.dram_tensor(k, v.shape, mybir.dt.from_np(v.dtype), kind="ExternalInput").ap()
            for k, v in arrays.items()]
    out = nc.dram_tensor("out", (T, D), F32, kind="ExternalOutput").ap()
    w_dram = nc.dram_tensor("w_scratch", (TILES, P, T - P), F32).ap()
    g_dram = nc.dram_tensor("g_scratch", (AHEAD, P, T), F32).ap()
    hybrid_layer(nc, *args, w_dram, g_dram, out)
    r = run_bass_kernel_spmd(nc, [arrays], core_ids=[0])
    return r.results[0]["out"].reshape(1, T, D)
```
